# Optimizing a Trainium2 kernel written in Bass

```python
import jax, jax.numpy as jnp
from jax import lax
import numpy as np

D_MODEL = 1024
BATCH = 1
SEQ = 1024
DEPTH = 2
DEC_BATCH = 8
DEC_SEQ = 1
PAST_LEN = 4096
PAGE_SIZE = 128

HEAD_DIM = 64
N_HEADS = 8
N_KV = 2
GQA_G = N_HEADS // N_KV
WINDOW = 128
BLK = WINDOW
ROPE_THETA = 10000.0
R_HEADS = 4
R_DK = 128
R_DV = 128
HGRN_CHUNK = 64
ATTN_W = N_HEADS * HEAD_DIM
KV_W = N_KV * HEAD_DIM
R_KW = R_HEADS * R_DK
R_VW = R_HEADS * R_DV
MIX_W = ATTN_W + R_VW
P_IN = ATTN_W + 2 * KV_W + 2 * R_KW + 2 * R_VW
N_MEM = 256
X_HEADS = 4
X_HEAD_DIM = D_MODEL // X_HEADS
D_FF = 2816
CONV_W = 3
EPS = 1e-6

kernel_name = 'hymba_swa_hgrn2_memxattn_convffn_step'

def rms_norm(x, g):
    x32 = x.astype(jnp.float32)
    y = x32 * lax.rsqrt(jnp.mean(x32 * x32, axis=-1, keepdims=True) + EPS)
    return (y * g.astype(jnp.float32)).astype(x.dtype)

def rope(x, pos):
    half = HEAD_DIM // 2
    inv_freq = ROPE_THETA ** (-jnp.arange(half, dtype=jnp.float32) / half)
    ang = pos.astype(jnp.float32)[:, None] * inv_freq[None, :]
    cos = jnp.cos(ang)[None, :, None, :]
    sin = jnp.sin(ang)[None, :, None, :]
    x32 = x.astype(jnp.float32)
    x1, x2 = x32[..., :half], x32[..., half:]
    return jnp.concatenate([x1 * cos - x2 * sin, x2 * cos + x1 * sin], axis=-1).astype(x.dtype)

def sink_attention(q, k, v, mask, sink):
    s = jnp.einsum('...qkgd,...skd->...kgqs', q.astype(jnp.float32), k.astype(jnp.float32)) * (HEAD_DIM ** -0.5)
    s = jnp.where(mask, s, -jnp.inf)
    sk = sink.astype(jnp.float32)[..., None, None]
    m = jnp.maximum(jnp.max(s, axis=-1, keepdims=True), sk)
    p = jnp.exp(s - m)
    p = p / (jnp.sum(p, axis=-1, keepdims=True) + jnp.exp(sk - m))
    return jnp.einsum('...kgqs,...skd->...qkgd', p, v.astype(jnp.float32))

def swa_prompt(q, k, v, sink):
    B, L = q.shape[0], q.shape[1]
    nb = L // BLK
    qb = q.reshape(B, nb, BLK, N_KV, GQA_G, HEAD_DIM)
    pad = ((0, 0), (BLK, 0), (0, 0), (0, 0))
    kp = jnp.pad(k, pad).reshape(B, nb + 1, BLK, N_KV, HEAD_DIM)
    vp = jnp.pad(v, pad).reshape(B, nb + 1, BLK, N_KV, HEAD_DIM)
    kb = jnp.concatenate([kp[:, :-1], kp[:, 1:]], axis=2)
    vb = jnp.concatenate([vp[:, :-1], vp[:, 1:]], axis=2)
    qpos = jnp.arange(nb)[:, None] * BLK + jnp.arange(BLK)[None, :]
    kpos = jnp.arange(nb)[:, None] * BLK - BLK + jnp.arange(2 * BLK)[None, :]
    diff = qpos[:, :, None] - kpos[:, None, :]
    mask = (diff >= 0) & (diff <= WINDOW) & (kpos[:, None, :] >= 0)
    mask = mask[None, :, None, None]
    o = sink_attention(qb, kb, vb, mask, sink.reshape(N_KV, GQA_G))
    return o.reshape(B, L, ATTN_W)

def swa_sample(q, k, v, buf_k, buf_v, pos, sink):
    DB, L = q.shape[0], q.shape[1]
    W = buf_k.shape[1]
    kk = jnp.concatenate([buf_k.astype(k.dtype), k], axis=1)
    vv = jnp.concatenate([buf_v.astype(v.dtype), v], axis=1)
    kpos = jnp.concatenate([pos[0] - W + jnp.arange(W, dtype=jnp.int32), pos])
    diff = pos[:, None] - kpos[None, :]
    mask = (diff >= 0) & (diff <= WINDOW)
    o = sink_attention(q.reshape(DB, L, N_KV, GQA_G, HEAD_DIM), kk, vv, mask, sink.reshape(N_KV, GQA_G))
    return o.reshape(DB, L, ATTN_W)

def hgrn_chunked(q, g, k, v, s0, chunk):
    B, L = q.shape[0], q.shape[1]
    n = L // chunk

    def to_chunks(t):
        return jnp.moveaxis(t.reshape(B, n, chunk, t.shape[2], t.shape[3]), 1, 0)

    tril = jnp.tril(jnp.ones((chunk, chunk), dtype=bool))[None, :, :, None, None]

    def step(S, inp):
        qc, gc, kc, vc = inp
        b = jnp.cumsum(gc, axis=1)
        dec = jnp.exp(jnp.where(tril, b[:, :, None] - b[:, None, :], -jnp.inf))
        att = jnp.einsum('btshk,bshk->bhts', qc[:, :, None] * dec, kc)
        o = jnp.einsum('bhts,bshv->bthv', att, vc) + jnp.einsum('bthk,bhkv->bthv', qc * jnp.exp(b), S)
        b_last = b[:, -1]
        S = jnp.exp(b_last)[..., None] * S + jnp.einsum('bshk,bshv->bhkv', kc * jnp.exp(b_last[:, None] - b), vc)
        return S, o

    S, o = lax.scan(step, s0, (to_chunks(q), to_chunks(g), to_chunks(k), to_chunks(v)))
    o = jnp.moveaxis(o, 0, 1).reshape(B, L, R_HEADS, R_DV)
    return o, S

def hgrn_branch(qr, fr, ir, gr, lb_l, gn_l, s0, chunk):
    B, L = qr.shape[0], qr.shape[1]
    lb = lb_l.reshape(R_HEADS, R_DK)
    z = fr.astype(jnp.float32).reshape(B, L, R_HEADS, R_DK)
    logf = jnp.logaddexp(jnp.log(lb), jnp.log1p(-lb) + jax.nn.log_sigmoid(z))
    k = (1.0 - lb) * jax.nn.sigmoid(-z)
    q = jax.nn.silu(qr.astype(jnp.float32)).reshape(B, L, R_HEADS, R_DK)
    v = ir.astype(jnp.float32).reshape(B, L, R_HEADS, R_DV)
    o, S = hgrn_chunked(q, logf, k, v, s0, chunk)
    o = o * lax.rsqrt(jnp.mean(o * o, axis=-1, keepdims=True) + EPS) * gn_l.astype(jnp.float32).reshape(R_HEADS, R_DV)
    o = o.reshape(B, L, R_VW) * jax.nn.silu(gr.astype(jnp.float32))
    return o, S

def token_mixer(h, pos, w_in_l, w_o_l, sink_l, lb_l, gn_l, s0, chunk, buf_k, buf_v):
    B, L = h.shape[0], h.shape[1]
    proj = h @ w_in_l
    offs = [ATTN_W, ATTN_W + KV_W, ATTN_W + 2 * KV_W, ATTN_W + 2 * KV_W + R_KW,
            ATTN_W + 2 * KV_W + 2 * R_KW, ATTN_W + 2 * KV_W + 2 * R_KW + R_VW]
    qa, ka, va, qr, fr, ir, gr = jnp.split(proj, offs, axis=-1)
    qa = rope(qa.reshape(B, L, N_HEADS, HEAD_DIM), pos)
    ka = rope(ka.reshape(B, L, N_KV, HEAD_DIM), pos)
    va = va.reshape(B, L, N_KV, HEAD_DIM)
    if buf_k is None:
        attn = swa_prompt(qa, ka, va, sink_l)
    else:
        attn = swa_sample(qa, ka, va, buf_k, buf_v, pos, sink_l)
    rec, S = hgrn_branch(qr, fr, ir, gr, lb_l, gn_l, s0, chunk)
    mixed = jnp.concatenate([attn, rec], axis=-1).astype(h.dtype) @ w_o_l
    return mixed, ka, va, S

def cross_attention(h, mk, mv, w_xq_l, w_xo_l):
    B, L = h.shape[0], h.shape[1]
    q = (h @ w_xq_l).reshape(B, L, X_HEADS, X_HEAD_DIM)
    s = jnp.einsum('bqhd,bmhd->bhqm', q.astype(jnp.float32), mk.astype(jnp.float32)) * (X_HEAD_DIM ** -0.5)
    p = jax.nn.softmax(s, axis=-1)
    o = jnp.einsum('bhqm,bmhd->bqhd', p, mv.astype(jnp.float32))
    return o.reshape(B, L, D_MODEL).astype(h.dtype) @ w_xo_l

def conv_ffn(h, w_up_l, conv_w_l, conv_b_l, w_down_l, buf):
    u = h @ w_up_l
    L = u.shape[1]
    up = jnp.concatenate([buf.astype(u.dtype), u], axis=1)
    c = conv_b_l
    for j in range(CONV_W):
        c = c + up[:, j:j + L] * conv_w_l[j]
    a, b = jnp.split(c, 2, axis=-1)
    y = (jax.nn.silu(a) * b) @ w_down_l
    return y, up[:, -(CONV_W - 1):]

def setup_inputs(seed: int = 0) -> dict:
    key = jax.random.key(seed)
    ks = jax.random.split(key, 32)
    nrm = jax.random.normal
    f32 = jnp.float32
    w_buf = min(WINDOW, PAST_LEN)

    def gain(k, shape):
        return 1.0 + 0.05 * nrm(k, shape, f32)

    return {
        'x_prompt': nrm(ks[0], (BATCH, SEQ, D_MODEL), f32),
        'x_sample': nrm(ks[1], (DEC_BATCH, DEC_SEQ, D_MODEL), f32),
        'cache_win_k': nrm(ks[2], (DEPTH, DEC_BATCH, w_buf, N_KV, HEAD_DIM), f32),
        'cache_win_v': nrm(ks[3], (DEPTH, DEC_BATCH, w_buf, N_KV, HEAD_DIM), f32),
        'cache_mem_k': nrm(ks[4], (DEPTH, DEC_BATCH, N_MEM, X_HEADS, X_HEAD_DIM), f32),
        'cache_mem_v': nrm(ks[5], (DEPTH, DEC_BATCH, N_MEM, X_HEADS, X_HEAD_DIM), f32),
        'state_hgrn': 0.3 * nrm(ks[6], (DEPTH, DEC_BATCH, R_HEADS, R_DK, R_DV), f32),
        'cache_ffn_conv': nrm(ks[7], (DEPTH, DEC_BATCH, CONV_W - 1, 2 * D_FF), f32),
        'mem_prompt': nrm(ks[8], (BATCH, N_MEM, D_MODEL), f32),
        'w_in': nrm(ks[9], (DEPTH, D_MODEL, P_IN), f32) * D_MODEL ** -0.5,
        'w_o': nrm(ks[10], (DEPTH, MIX_W, D_MODEL), f32) * MIX_W ** -0.5,
        'attn_sinks': 0.5 * nrm(ks[11], (DEPTH, N_HEADS), f32),
        'lb_logits': 0.5 * nrm(ks[12], (DEPTH, R_KW), f32),
        'hgrn_norm': gain(ks[13], (DEPTH, R_VW)),
        'w_xq': nrm(ks[14], (DEPTH, D_MODEL, D_MODEL), f32) * D_MODEL ** -0.5,
        'w_xk': nrm(ks[15], (DEPTH, D_MODEL, D_MODEL), f32) * D_MODEL ** -0.5,
        'w_xv': nrm(ks[16], (DEPTH, D_MODEL, D_MODEL), f32) * D_MODEL ** -0.5,
        'w_xo': nrm(ks[17], (DEPTH, D_MODEL, D_MODEL), f32) * D_MODEL ** -0.5,
        'w_up': nrm(ks[18], (DEPTH, D_MODEL, 2 * D_FF), f32) * D_MODEL ** -0.5,
        'conv_w': nrm(ks[19], (DEPTH, CONV_W, 2 * D_FF), f32) * CONV_W ** -0.5,
        'conv_b': 0.02 * nrm(ks[20], (DEPTH, 2 * D_FF), f32),
        'w_down': nrm(ks[21], (DEPTH, D_FF, D_MODEL), f32) * D_FF ** -0.5,
        'g_pre_mix': gain(ks[22], (DEPTH, D_MODEL)),
        'g_post_mix': gain(ks[23], (DEPTH, D_MODEL)),
        'g_pre_x': gain(ks[24], (DEPTH, D_MODEL)),
        'g_post_x': gain(ks[25], (DEPTH, D_MODEL)),
        'g_mem': gain(ks[26], (DEPTH, D_MODEL)),
        'g_pre_ffn': gain(ks[27], (DEPTH, D_MODEL)),
        'g_post_ffn': gain(ks[28], (DEPTH, D_MODEL)),
    }

def reference(x_prompt, x_sample, cache_win_k, cache_win_v, cache_mem_k, cache_mem_v, state_hgrn, cache_ffn_conv,
              mem_prompt, w_in, w_o, attn_sinks, lb_logits, hgrn_norm, w_xq, w_xk, w_xv, w_xo, w_up, conv_w, conv_b,
              w_down, g_pre_mix, g_post_mix, g_pre_x, g_post_x, g_mem, g_pre_ffn, g_post_ffn):
    c = jnp.cumsum(jax.nn.softmax(lb_logits.astype(jnp.float32), axis=0), axis=0)
    lb = c - c[0:1]

    xp, xs = x_prompt, x_sample
    Bp, Lp = xp.shape[0], xp.shape[1]
    Ls = xs.shape[1]
    pos_p = jnp.arange(Lp, dtype=jnp.int32)
    pos_s = PAST_LEN + jnp.arange(Ls, dtype=jnp.int32)
    n_keep = min(WINDOW, Lp)
    chunk_p = min(HGRN_CHUNK, Lp)

    wkp, wvp, wks, wvs, mkp, mvp, hsp, hss, cvp, cvs = [], [], [], [], [], [], [], [], [], []
    for l in range(DEPTH):
        mp, kp_, vp_, Sp = token_mixer(rms_norm(xp, g_pre_mix[l]), pos_p, w_in[l], w_o[l], attn_sinks[l], lb[l],
                                       hgrn_norm[l], jnp.zeros((Bp, R_HEADS, R_DK, R_DV), jnp.float32), chunk_p,
                                       None, None)
        xp = xp + rms_norm(mp, g_post_mix[l])
        ms, ks_, vs_, Ss = token_mixer(rms_norm(xs, g_pre_mix[l]), pos_s, w_in[l], w_o[l], attn_sinks[l], lb[l],
                                       hgrn_norm[l], state_hgrn[l].astype(jnp.float32), Ls,
                                       cache_win_k[l], cache_win_v[l])
        xs = xs + rms_norm(ms, g_post_mix[l])
        wkp.append(kp_[:, -n_keep:])
        wvp.append(vp_[:, -n_keep:])
        wks.append(ks_)
        wvs.append(vs_)
        hsp.append(Sp.astype(x_prompt.dtype))
        hss.append(Ss.astype(state_hgrn.dtype))

        hm = rms_norm(mem_prompt, g_mem[l])
        mk = (hm @ w_xk[l]).reshape(Bp, N_MEM, X_HEADS, X_HEAD_DIM)
        mv = (hm @ w_xv[l]).reshape(Bp, N_MEM, X_HEADS, X_HEAD_DIM)
        xp = xp + rms_norm(cross_attention(rms_norm(xp, g_pre_x[l]), mk, mv, w_xq[l], w_xo[l]), g_post_x[l])
        xs = xs + rms_norm(cross_attention(rms_norm(xs, g_pre_x[l]), cache_mem_k[l], cache_mem_v[l], w_xq[l],
                                           w_xo[l]), g_post_x[l])
        mkp.append(mk)
        mvp.append(mv)

        fp, bufp = conv_ffn(rms_norm(xp, g_pre_ffn[l]), w_up[l], conv_w[l], conv_b[l], w_down[l],
                            jnp.zeros((Bp, CONV_W - 1, 2 * D_FF), xp.dtype))
        xp = xp + rms_norm(fp, g_post_ffn[l])
        fs, bufs = conv_ffn(rms_norm(xs, g_pre_ffn[l]), w_up[l], conv_w[l], conv_b[l], w_down[l], cache_ffn_conv[l])
        xs = xs + rms_norm(fs, g_post_ffn[l])
        cvp.append(bufp)
        cvs.append(bufs)

    y_prompt, y_sample = xp, xs
    win_k_prompt, win_v_prompt = jnp.stack(wkp), jnp.stack(wvp)
    win_k_sample, win_v_sample = jnp.stack(wks), jnp.stack(wvs)
    mem_k_prompt, mem_v_prompt = jnp.stack(mkp), jnp.stack(mvp)
    hgrn_prompt, hgrn_sample = jnp.stack(hsp), jnp.stack(hss)
    conv_prompt, conv_sample = jnp.stack(cvp), jnp.stack(cvs)
    return (y_prompt, y_sample, win_k_prompt, win_v_prompt, win_k_sample, win_v_sample, mem_k_prompt, mem_v_prompt,
            hgrn_prompt, hgrn_sample, conv_prompt, conv_sample)


_drawn_inputs = setup_inputs


def setup_inputs(seed=0):
    import zlib

    import numpy as np

    out = dict(_drawn_inputs(seed))
    spreads = {}
    factors = {'attn_sinks': 5.726, 'conv_b': 2.79}
    for name, (base, spread) in spreads.items():
        noise = np.random.default_rng([zlib.crc32(name.encode()), seed]).standard_normal(out[name].shape)
        drawn = base * np.exp(spread * noise) if base else spread * noise
        out[name] = __import__('jax').numpy.asarray(drawn.astype(out[name].dtype))
    for name, factor in factors.items():
        out[name] = (out[name] * factor).astype(out[name].dtype)
    return out
```

```python
from contextlib import ExitStack

import numpy as np

import concourse.bass as bass
from concourse import mybir

F32 = mybir.dt.float32
F32R = mybir.dt.float32r
BF16 = mybir.dt.bfloat16
U8 = mybir.dt.uint8
ALU = mybir.AluOpType
ACT = mybir.ActivationFunctionType
AX = mybir.AxisListType

P = 128
D = 1024
SEQ = 1024
NS = 8
T = SEQ + NS
NCH = 3
CH = T // NCH
DEPTH = 2
KT = D // P
HD = 64
NH = 8
NKV = 2
G = NH // NKV
PAST = 4096
WINDOW = 128
NB = SEQ // P
RH = 4
LEVELS = 7
NMEM = 256
XH = 4
DFF = 2816
FT = DFF // P
P_IN = 2816
EPS = 1e-6
F_FLOOR = 1e-18
NEG = -1e30

N_QKV, N_HGRN, N_WO, N_MEM, N_XQ, N_XO, N_FFN = 6, 16, 8, 16, 8, 8, 3 * FT
S_HGRN = 0
S_QKV = S_HGRN + N_HGRN
S_WO = S_QKV + N_QKV
S_MEM = S_WO + N_WO
S_XQ = S_MEM + N_MEM
S_XO = S_XQ + N_XQ
S_FFN = S_XO + N_XO
N_SLABS = S_FFN + N_FFN

G_PRE_MIX, G_POST_MIX, G_PRE_X, G_POST_X, G_MEM, G_PRE_FFN, G_POST_FFN, G_HGRN = [8 * i for i in range(8)]
N_GROWS = 8 * 7 + 4
ROPE_HALF = HD // 2


class Chain:

    def __init__(self, sem):
        self.sem, self.n, self.eng = sem, 0, None

    def __call__(self, ins):
        self.n += 1
        ins.then_inc(self.sem, 1)
        self.eng.wait_ge(self.sem, self.n)


def build_program(nc, io):
    ctx = ExitStack()
    with ctx:
        def sb(name, shape, dt=F32):
            return ctx.enter_context(nc.sbuf_tensor(name, shape, dt))

        lasting, passing = [], []
        stage_sems = ctx.enter_context(ExitStack())

        def lasting_sem(name):
            lasting.append(ctx.enter_context(nc.semaphore(name)))
            return lasting[-1]

        def sem(name):
            passing.append(stage_sems.enter_context(nc.semaphore(name)))
            return passing[-1]

        xT = sb("xT", [P, KT, T])
        hh = sb("hh", [P, KT, T], F32R)
        hl = sb("hl", [P, KT, T], F32R)
        Y = sb("Y", [P, KT, T])
        w_raw = sb("w_raw", [P, 2, 1024])
        w_hi = sb("w_hi", [P, 2, 1024], F32R)
        w_lo = sb("w_lo", [P, 2, 1024], F32R)
        rs = sb("rs", [P, T])
        gT = sb("gT", [P, N_GROWS])
        cT = sb("cT", [P, 4, 2 * FT])
        ident = sb("ident", [P, P])
        ones = sb("ones", [P, P])
        swa_mask = sb("swa_mask", [P, 2 * P])
        lvl_mask = sb("lvl_mask", [P, LEVELS, P], U8)
        restart = sb("restart", [P, SEQ], BF16)
        LB = sb("LB", [P, DEPTH, RH])
        lbt = sb("lbt", [P, RH])
        oml = sb("oml", [P, RH])
        epst = sb("epst", [P, 1])
        ps = ctx.enter_context(nc.psum_tensor("ps", [P, 8, 512], F32))

        raw_loaded = [lasting_sem("raw_loaded0"), lasting_sem("raw_loaded1")]
        hi_done = lasting_sem("hi_done")
        lo_done = lasting_sem("lo_done")
        w_used = lasting_sem("w_used")
        act_c, dve_c, pe_c, pool_c = (Chain(lasting_sem(n)) for n in ("act_step", "dve_step", "pe_step", "pool_step"))
        done = {"raw": 0, "hi": 0, "lo": 0}

        def slab_source(l, n):
            def cols(w, c0):
                return [(slice(0, P), None, w[l].rearrange("(k p) f -> p k f", p=P)[:, :, c0:c0 + P])]
            if n < S_QKV:
                r, part = divmod(n, 4)
                return cols(io["w_in"], 768 + 512 * part + P * r)
            if n < S_QKV + G:
                j = n - S_QKV
                w = io["w_in"][l].rearrange("(k p) f -> p k f", p=P)
                return [(slice(0, P), lambda s, g=g: s.rearrange("p (k f) -> p k f", k=KT)[:, :, HD * g:HD * g + HD],
                         w[:, :, 256 * g + HD * j:256 * g + HD * j + HD]) for g in range(2)]
            if n < S_WO:
                return cols(io["w_in"], P * (n - S_QKV))
            if n < S_MEM:
                c0 = P * (n - S_WO)
                w = io["w_o"][l]
                parts = []
                for g in range(2):
                    rows = w[256 * g:256 * g + 256, c0:c0 + P].rearrange("(j p) f -> p j f", p=HD)
                    parts.append((slice(HD * g, HD * g + HD),
                                  lambda s: s.rearrange("p (k f) -> p k f", k=KT)[:, 0:4, :], rows))
                parts.append((slice(0, P), lambda s: s.rearrange("p (k f) -> p k f", k=KT)[:, 4:8, :],
                              w[512:1024, c0:c0 + P].rearrange("(j p) f -> p j f", p=P)))
                return parts
            if n < S_XQ:
                which, k = divmod(n - S_MEM, KT)
                return [(slice(0, P), lambda s: s, io[("w_xk", "w_xv")[which]][l][P * k:P * k + P, :])]
            if n < S_XO:
                return cols(io["w_xq"], P * (n - S_XQ))
            if n < S_FFN:
                return cols(io["w_xo"], P * (n - S_XO))
            kind, j = ffn_order[n - S_FFN]
            if kind == "d":
                return [(slice(0, P), lambda s: s, io["w_down"][l][P * j:P * j + P, :])]
            return cols(io["w_up"], P * j + (DFF if kind == "b" else 0))

        ffn_order = [("a", 0), ("b", 0)]
        for j in range(1, FT):
            ffn_order += [("a", j), ("b", j), ("d", j - 1)]
        ffn_order += [("d", FT - 1)]

        def load_slabs(eng, l, upto):
            for n in range(done["raw"], min(upto, N_SLABS)):
                if n >= 2:
                    eng.wait_ge(lo_done, n - 1)
                parts = slab_source(l, n)
                for i, (pp, view, src) in enumerate(parts):
                    dst = w_raw[pp, n % 2, :]
                    dst = view(dst) if view else dst.rearrange("p (k f) -> p k f", k=KT)
                    inc = 48 - 16 * (len(parts) - 1) if i == 0 else 16
                    eng.dma_start(dst, src).then_inc(raw_loaded[n % 2], inc)
            done["raw"] = max(done["raw"], min(upto, N_SLABS))

        def split_hi(eng, upto):
            for n in range(done["hi"], min(upto, N_SLABS)):
                eng.wait_ge(raw_loaded[n % 2], 48 * (n // 2 + 1))
                if n >= 2:
                    eng.wait_ge(w_used, n - 1)
                nc.scalar.activation(w_hi[:, n % 2, :], w_raw[:, n % 2, :], ACT.Copy).then_inc(hi_done, 1)
            done["hi"] = max(done["hi"], min(upto, N_SLABS))

        def split_lo(eng, upto):
            for n in range(done["lo"], min(upto, N_SLABS)):
                eng.wait_ge(hi_done, n + 1)
                nc.gpsimd.tensor_tensor(w_lo[:, n % 2, :], w_raw[:, n % 2, :], w_hi[:, n % 2, :].bitcast(F32),
                                        ALU.subtract).then_inc(lo_done, 1)
            done["lo"] = max(done["lo"], min(upto, N_SLABS))

        def mm3(out, whi, wlo, mhi, mlo, start, stop):
            nc.tensor.matmul(out, whi, mhi, start=start, stop=False)
            nc.tensor.matmul(out, whi, mlo, start=False, stop=False)
            return nc.tensor.matmul(out, wlo, mhi, start=False, stop=stop)

        def project(pe, n, bank):
            pe.wait_ge(lo_done, n + 1)
            s = n % 2
            for c in range(NCH):
                for k in range(KT):
                    last = mm3(ps[:, bank + c, 0:CH], w_hi[:, s, P * k:P * k + P], w_lo[:, s, P * k:P * k + P],
                               hh[:, k, CH * c:CH * c + CH], hl[:, k, CH * c:CH * c + CH], k == 0, k == KT - 1)
            last.then_inc(w_used, 1)

        def tokens3(ap):
            return ap.rearrange("p (c t) -> p c t", c=NCH)

        def over_heads(ap, n):
            return ap.unsqueeze(1).to_broadcast([ap.shape[0], n, ap.shape[1]])

        def over_cols(ap, n):
            return ap.unsqueeze(2).to_broadcast([ap.shape[0], ap.shape[1], n])

        def clear_semaphores(all_of_them):
            nc.all_engine_barrier()
            with nc.Block() as block:
                @block.sync
                def _(sp):
                    for s in passing + (lasting if all_of_them else []):
                        sp.sem_clear(s)
            nc.all_engine_barrier()
            passing.clear()
            stage_sems.close()
            if all_of_them:
                for c in (act_c, dve_c, pe_c, pool_c):
                    c.n = 0
                for key in done:
                    done[key] = 0

        with ExitStack() as ph:
            def tmp(name, shape, dt=F32):
                return ph.enter_context(nc.sbuf_tensor(name, shape, dt))

            rows = tmp("x_rows", [P, 3, D])
            lvl_f = tmp("lvl_mask_f", [P, LEVELS, P])
            lrow = tmp("lb_rows", [DEPTH * RH, P])
            lg = tmp("lb_cols", [P, DEPTH, RH])
            lm = tmp("lb_max", [P, RH])
            le = tmp("lb_exp", [P, DEPTH, RH])
            consts_in, rows_in, rows_done = sem("consts_in"), [sem(f"rows_in{i}") for i in range(3)], sem("rows_done")
            x_copied, lb_in, lb_ready, lb_sub, lb_exped = (sem(n) for n in (
                "x_copied", "lb_in", "lb_ready", "lb_sub", "lb_exped"))
            n_tiles = NB + 1

            def row_tile(i):
                return (P, io["x_prompt"][0, P * i:P * i + P, :]) if i < NB else (NS, io["x_sample"][:, 0, :])

            with nc.Block() as block:
                @block.sync
                def _(sp):
                    sp.dma_start(ident[:], io["c_ident"]).then_inc(consts_in, 16)
                    sp.dma_start(swa_mask[:], io["c_swa"]).then_inc(consts_in, 16)
                    sp.dma_start(lvl_f[:], io["c_lvl"]).then_inc(consts_in, 16)
                    sp.dma_start(lrow[:], io["lb_logits"].rearrange("l (r p) -> (l r) p", p=P)).then_inc(lb_in, 16)
                    for i in range(n_tiles):
                        if i >= 3:
                            sp.wait_ge(rows_done, i - 2)
                        m, src = row_tile(i)
                        sp.dma_start(rows[0:m, i % 3, :], src).then_inc(rows_in[i % 3], 16)

                @block.tensor
                def _(pe):
                    pe.wait_ge(consts_in, 48)
                    for i in range(n_tiles):
                        pe.wait_ge(rows_in[i % 3], 16 * (i // 3 + 1))
                        if i >= 2:
                            pe.wait_ge(x_copied, i - 1)
                        m, _ = row_tile(i)
                        for k in range(KT):
                            last = nc.tensor.transpose(ps[:, 2 * (i % 2) + k // 4, P * (k % 4):P * (k % 4) + m],
                                                       rows[0:m, i % 3, P * k:P * k + P], ident[0:m, 0:m])
                        last.then_inc(rows_done, 1)
                    pe.wait_ge(lb_in, 16)
                    nc.tensor.transpose(ps[:, 7, 0:DEPTH * RH], lrow[:],
                                        ident[0:DEPTH * RH, 0:DEPTH * RH]).then_inc(lb_ready, 1)

                @block.scalar
                def _(act):
                    for i in range(n_tiles):
                        act.wait_ge(rows_done, i + 1)
                        m, _ = row_tile(i)
                        for h in range(2):
                            src = ps[:, 2 * (i % 2) + h, :].rearrange("p (k t) -> p k t", k=4)[:, :, 0:m]
                            last = nc.scalar.activation(xT[:, 4 * h:4 * h + 4, P * i:P * i + m], src, ACT.Copy)
                        last.then_inc(x_copied, 1)
                    act.wait_ge(lb_sub, 1)
                    nc.scalar.activation(le[:], lg[:], ACT.Exp).then_inc(lb_exped, 1)

                @block.vector
                def _(dve):
                    dve_c.eng = dve
                    dve_c(nc.vector.memset(ones[:], 1.0))
                    dve_c(nc.vector.memset(epst[:], EPS))
                    dve_c(nc.vector.memset(restart[:], 1.0))
                    dve_c(nc.vector.memset(restart[:].rearrange("p (c t) -> p c t", t=P)[:, :, 0:1], 0.0))
                    dve.wait_ge(consts_in, 48)
                    dve_c(nc.vector.tensor_copy(lvl_mask[:], lvl_f[:]))
                    dve.wait_ge(lb_ready, 1)
                    dve_c(nc.vector.tensor_copy(lg[:].rearrange("p l r -> p (l r)"), ps[:, 7, 0:DEPTH * RH]))
                    dve_c(nc.vector.tensor_tensor(lm[:], lg[:, 0, :], lg[:, 1, :], ALU.max))
                    nc.vector.tensor_tensor(lg[:], lg[:], over_heads(lm[:], DEPTH), ALU.subtract).then_inc(lb_sub, 1)
                    dve.wait_ge(lb_exped, 1)
                    dve_c(nc.vector.tensor_tensor(lm[:], le[:, 0, :], le[:, 1, :], ALU.add))
                    dve_c(nc.vector.reciprocal(lm[:], lm[:]))
                    dve_c(nc.vector.memset(LB[:, 0, :], 0.0))
                    dve_c(nc.vector.tensor_tensor(LB[:, 1, :], le[:, 1, :], lm[:], ALU.mult))

        def stage_parameters(l):
            with ExitStack() as ph:
                grow = ph.enter_context(nc.sbuf_tensor("g_rows", [N_GROWS, P], F32))
                crow = ph.enter_context(nc.sbuf_tensor("c_rows", [2 * FT, 4, P], F32))
                g_in, c_in, gc_ready = sem("g_in"), sem("c_in"), sem("gc_ready")
                with nc.Block() as block:
                    @block.sync
                    def _(sp):
                        load_slabs(sp, l, 2)

                    @block.scalar
                    def _(act):
                        for i, g in enumerate(("g_pre_mix", "g_post_mix", "g_pre_x", "g_post_x", "g_mem",
                                               "g_pre_ffn", "g_post_ffn")):
                            act.dma_start(grow[8 * i:8 * i + 8, :], io[g][l].rearrange("(k p) -> k p", p=P)).then_inc(g_in, 16)
                        act.dma_start(grow[G_HGRN:G_HGRN + 4, :],
                                      io["hgrn_norm"][l].rearrange("(k p) -> k p", p=P)).then_inc(g_in, 16)
                        for j in range(3):
                            act.dma_start(crow[:, j, :], io["conv_w"][l, j].rearrange("(k p) -> k p", p=P)).then_inc(c_in, 16)
                        act.dma_start(crow[:, 3, :], io["conv_b"][l].rearrange("(k p) -> k p", p=P)).then_inc(c_in, 16)

                    @block.tensor
                    def _(pe):
                        pe.wait_ge(g_in, 16 * 8)
                        nc.tensor.transpose(ps[:, 0, 0:N_GROWS], grow[:], ident[0:N_GROWS, 0:N_GROWS])
                        pe.wait_ge(c_in, 16 * 4)
                        for j in range(4):
                            last = nc.tensor.transpose(ps[:, 1, 2 * FT * j:2 * FT * j + 2 * FT], crow[:, j, :],
                                                       ident[0:2 * FT, 0:2 * FT])
                        last.then_inc(gc_ready, 1)

                    @block.vector
                    def _(dve):
                        dve_c.eng = dve
                        dve.wait_ge(gc_ready, 1)
                        dve_c(nc.vector.tensor_copy(gT[:], ps[:, 0, 0:N_GROWS]))
                        dve_c(nc.vector.tensor_copy(cT[:].rearrange("p j k -> p (j k)"), ps[:, 1, 0:8 * FT]))
                        dve_c(nc.vector.tensor_copy(lbt[:], LB[:, l, :]))
                        dve_c(nc.vector.tensor_scalar(oml[:], lbt[:], -1.0, 1.0, ALU.mult, ALU.add))
                        dve_c(nc.vector.tensor_scalar(lbt[:], lbt[:], F_FLOOR, None, ALU.add))

        def stage_norm(name, l, post, pre, next_slab):
            with ExitStack() as ph:
                sq = [ph.enter_context(nc.sbuf_tensor(f"{name}_sq{i}", [P, KT, CH], F32)) for i in range(2)]
                rt = ph.enter_context(nc.sbuf_tensor(f"{name}_rt", [P, 2, CH], F32))
                rp = ph.enter_context(nc.sbuf_tensor(f"{name}_rp", [P, CH], F32))
                sq_ready, mean_ready, rt_ready, rt_used, x_ready, hh_ready = (
                    sem(f"{name}_{s}") for s in ("sq", "mean", "root", "rt_used", "x", "hh"))
                runs = [("post", c) for c in range(NCH)] * (post is not None)
                runs += [("pre", c) for c in range(NCH)] * (pre is not None)
                n_post = NCH * (post is not None)

                def chunk(t, c):
                    return t[:, :, CH * c:CH * c + CH]

                with nc.Block() as block:
                    @block.sync
                    def _(sp):
                        load_slabs(sp, l, next_slab + 2)

                    @block.gpsimd
                    def _(pool):
                        split_lo(pool, next_slab + 2)

                    @block.scalar
                    def _(act):
                        def square(i):
                            kind, c = runs[i]
                            if kind == "pre" and post is not None:
                                act.wait_ge(x_ready, c + 1)
                            if i >= 2:
                                act.wait_ge(mean_ready, i - 1)
                            src = chunk(Y if kind == "post" else xT, c)
                            nc.scalar.activation(sq[i % 2][:], src, ACT.Square).then_inc(sq_ready, 1)

                        def root(i):
                            act.wait_ge(mean_ready, i + 1)
                            if i >= 2:
                                act.wait_ge(rt_used, i - 1)
                            nc.scalar.activation(rt[:, i % 2, :], ps[:, i % 2, 0:CH], ACT.Sqrt, bias=epst[:],
                                                 scale=1.0 / D).then_inc(rt_ready, 1)

                        def high(c):
                            if post is not None:
                                act.wait_ge(x_ready, c + 1)
                            for k in range(KT):
                                last = nc.scalar.activation(chunk(hh, c)[:, k, :], chunk(xT, c)[:, k, :], ACT.Copy,
                                                            scale=gT[:, pre + k:pre + k + 1])
                            last.then_inc(hh_ready, 1)

                        for i in range(n_post):
                            square(i)
                            if i:
                                root(i - 1)
                        if n_post:
                            root(n_post - 1)
                        if pre is not None:
                            for c in range(NCH):
                                high(c)
                                square(n_post + c)
                                if c:
                                    root(n_post + c - 1)
                            root(len(runs) - 1)
                        split_hi(act, next_slab + 2)

                    @block.tensor
                    def _(pe):
                        for i in range(len(runs)):
                            pe.wait_ge(sq_ready, i + 1)
                            if i >= 2:
                                pe.wait_ge(rt_ready, i - 1)
                            for k in range(KT):
                                last = nc.tensor.matmul(ps[:, i % 2, 0:CH], ones[:], sq[i % 2][:, k, :], start=(k == 0),
                                                        stop=(k == KT - 1))
                            last.then_inc(mean_ready, 1)

                    @block.vector
                    def _(dve):
                        dve_c.eng = dve

                        def apply(i, c):
                            dve.wait_ge(rt_ready, i + 1)
                            nc.vector.reciprocal(rp[:], rt[:, i % 2, :]).then_inc(rt_used, 1)
                            dve.wait_ge(rt_used, i + 1)
                            dve_c(nc.vector.tensor_tensor(chunk(Y, c), chunk(Y, c), over_heads(rp[:], KT), ALU.mult))
                            for k in range(KT):
                                last = nc.vector.scalar_tensor_tensor(
                                    chunk(xT, c)[:, k, :], chunk(Y, c)[:, k, :], gT[:, post + k:post + k + 1],
                                    chunk(xT, c)[:, k, :], ALU.mult, ALU.add)
                            last.then_inc(x_ready, 1)

                        def low(c):
                            dve.wait_ge(hh_ready, c + 1)
                            if post is not None:
                                dve.wait_ge(x_ready, c + 1)
                            for k in range(KT):
                                dve_c(nc.vector.scalar_tensor_tensor(
                                    chunk(hl, c)[:, k, :], chunk(xT, c)[:, k, :], gT[:, pre + k:pre + k + 1],
                                    chunk(hh, c)[:, k, :].bitcast(F32), ALU.mult, ALU.subtract))

                        def scale(i, c):
                            dve.wait_ge(rt_ready, i + 1)
                            nc.vector.reciprocal(rs[:, CH * c:CH * c + CH], rt[:, i % 2, :]).then_inc(rt_used, 1)

                        for i in range(n_post):
                            apply(i, i)
                        if pre is not None:
                            for c in range(NCH):
                                low(c)
                                if c:
                                    scale(n_post + c - 1, c - 1)
                            scale(len(runs) - 1, NCH - 1)
                        dve.wait_ge(rt_used, len(runs))

        def stage_qkv(l, q, kT, v):
            with ExitStack() as ph:
                def tmp(name, shape, dt=F32):
                    return ph.enter_context(nc.sbuf_tensor(name, shape, dt))

                sw = tmp("rope_swapped", [P, 2, T])
                cos, sin = tmp("rope_cos", [P, T]), tmp("rope_sin", [P, T])
                kw = tmp("k_window", [P, P])
                ks, vs = tmp("k_sample", [NS, P]), tmp("v_sample", [NS, P])
                qkv_out, sw_used, tables_in, w_rows, rows_copied, win_out = (sem(n) for n in (
                    "qkv_out", "sw_used", "tables_in", "w_rows", "rows_copied", "win_out"))
                swapped = [sem(f"swapped{i}") for i in range(2)]
                S0 = S_QKV
                order = [0, 1, 2, 3, 4]
                with nc.Block() as block:
                    @block.sync
                    def _(sp):
                        sp.dma_start(cos[:], io["c_cos"]).then_inc(tables_in, 16)
                        sp.dma_start(sin[:], io["c_sin"]).then_inc(tables_in, 16)
                        for i in range(N_QKV):
                            load_slabs(sp, l, S0 + 2 + i)
                            if i < 5:
                                sp.wait_ge(qkv_out, i + 1)
                                if i >= 2:
                                    sp.wait_ge(sw_used, i - 1)
                                for b in range(4):
                                    a = b ^ 1
                                    sp.dma_start(sw[32 * b:32 * b + 32, i % 2, :],
                                                 (Y[32 * a:32 * a + 32, i, :] if i < 4 else kT[32 * a:32 * a + 32, :])).then_inc(swapped[i % 2], 16)
                        load_slabs(sp, l, S0 + N_QKV + 2)
                        sp.wait_ge(rows_copied, 3)
                        sp.dma_start(io["win_k_prompt"][l, 0].rearrange("s k d -> s (k d)"), kw[:]).then_inc(win_out, 16)
                        sp.dma_start(io["win_k_sample"][l, :, 0].rearrange("b k d -> b (k d)"), ks[:]).then_inc(win_out, 16)
                        sp.dma_start(io["win_v_sample"][l, :, 0].rearrange("b k d -> b (k d)"), vs[:]).then_inc(win_out, 16)
                        sp.wait_ge(win_out, 48)

                    @block.gpsimd
                    def _(pool):
                        split_lo(pool, S0 + N_QKV)

                    @block.scalar
                    def _(act):
                        split_hi(act, S0 + N_QKV)
                        act.wait_ge(w_rows, 1)
                        nc.scalar.activation(kw[:], ps[:, 6, 0:P], ACT.Copy).then_inc(rows_copied, 1)
                        nc.scalar.activation(ks[:], ps[0:NS, 6, P:2 * P], ACT.Copy).then_inc(rows_copied, 1)
                        nc.scalar.activation(vs[:], ps[0:NS, 6, 2 * P:3 * P], ACT.Copy).then_inc(rows_copied, 1)

                    @block.tensor
                    def _(pe):
                        for i in range(N_QKV):
                            if i >= 2:
                                pe.wait_ge(qkv_out, i - 1)
                            project(pe, S0 + i, 3 * (i % 2))
                        pe.wait_ge(sw_used, 5)
                        pe.wait_ge(qkv_out, N_QKV)
                        nc.tensor.transpose(ps[:, 6, 0:P], kT[:, SEQ - P:SEQ], ident[:])
                        nc.tensor.transpose(ps[0:NS, 6, P:2 * P], kT[:, SEQ:T], ident[:])
                        nc.tensor.transpose(ps[0:NS, 6, 2 * P:3 * P], v[:, SEQ:T], ident[:]).then_inc(w_rows, 1)

                    @block.vector
                    def _(dve):
                        dve_c.eng = dve

                        def evacuate(i):
                            dve.wait_ge(w_used, S0 + i + 1)
                            dst = Y[:, i, :] if i < 4 else kT[:] if i == 4 else v[:]
                            nc.vector.tensor_tensor(tokens3(dst), ps[:, 3 * (i % 2):3 * (i % 2) + 3, 0:CH],
                                                    tokens3(rs[:]), ALU.mult).then_inc(qkv_out, 1)

                        def rope(i):
                            dve.wait_ge(swapped[i % 2], 64 * (i // 2 + 1))
                            raw = Y[:, i, :] if i < 4 else kT[:]
                            dve_c(nc.vector.tensor_tensor(raw, raw, cos[:], ALU.mult))
                            dve_c(nc.vector.tensor_tensor(sw[:, i % 2, :], sw[:, i % 2, :], sin[:], ALU.mult))
                            out = q[:, i, :] if i < 4 else kT[:]
                            nc.vector.tensor_tensor(out, raw, sw[:, i % 2, :], ALU.add).then_inc(sw_used, 1)

                        dve.wait_ge(tables_in, 32)
                        for i in range(N_QKV):
                            evacuate(i)
                            if i:
                                rope(i - 1)
                        dve.wait_ge(sw_used, 5)
        def attention_blocks(name, groups, scale, bufs, masked, next_load, score_mms, pv_mms, evacuate_out):
            S, PT, small = bufs
            sc_ready, sc_used, neg_ready, exp_ready, p_ready, turned, pt_ready, pv_done, o_used = (
                sem(f"{name}_{s}") for s in ("scores", "scores_used", "negmax", "exp", "probs", "turned", "turned_copied",
                                             "pv", "out_used"))
            n = len(groups)

            def cols(g):
                hs = groups[g]
                return P * hs[0], P * (hs[-1] + 1)

            def view(t, g):
                a, b = cols(g)
                return t[:, g % 2, :].rearrange("p (h k) -> p h k", h=4)[:, :, a:b]

            with nc.Block() as block:
                @block.sync
                def _(sp):
                    next_load(sp)

                @block.tensor
                def _(pe):
                    def scores(g):
                        if g >= 2:
                            pe.wait_ge(sc_used, g - 1)
                        sv = ps[:, 2 * (g % 2):2 * (g % 2) + 2, :].rearrange("p b (h k) -> p (b h) k", h=2)
                        score_mms(g, sv).then_inc(sc_ready, 1)

                    def turn(g):
                        pe.wait_ge(p_ready, g + 1)
                        if g:
                            pe.wait_ge(pt_ready, g)
                        for half in groups[g]:
                            for h in range(4):
                                last = nc.tensor.transpose(ps[:, 4 + half, P * h:P * h + P],
                                                           S[:, g % 2, 256 * h + P * half:256 * h + P * half + P], ident[:])
                        last.then_inc(turned, 1)

                    def values(g):
                        pe.wait_ge(pt_ready, g + 1)
                        pv_mms(pe, g, PT[:, g % 2, :].rearrange("p (a h q) -> p a h q", a=2, h=4), o_used).then_inc(pv_done, 1)

                    scores(0)
                    scores(1)
                    scores(2)
                    turn(0)
                    for g in range(n):
                        if g + 3 < n:
                            scores(g + 3)
                        if g + 1 < n:
                            turn(g + 1)
                        values(g)

                @block.vector
                def _(dve):
                    dve_c.eng = dve

                    def before(g):
                        dve.wait_ge(sc_ready, g + 1)
                        if g >= 2:
                            dve.wait_ge(turned, g - 1)
                        a, b = cols(g)
                        sv = ps[:, 2 * (g % 2):2 * (g % 2) + 2, :].rearrange("p b (h k) -> p (b h) k", h=2)[:, :, a:b]
                        if masked is not None:
                            mask, sinks = masked
                            nc.vector.scalar_tensor_tensor(view(S, g), sv, scale, over_heads(mask[:, a:b], 4), ALU.mult,
                                                           ALU.add).then_inc(sc_used, 1)
                        else:
                            nc.vector.tensor_scalar(view(S, g), sv, scale, None, ALU.mult).then_inc(sc_used, 1)
                        dve.wait_ge(sc_used, g + 1)
                        st = small[:, g % 2]
                        dve_c(nc.vector.tensor_reduce(st[:, 0, :], view(S, g), AX.X, ALU.max))
                        if masked is not None:
                            sk = sinks(g)
                            dve_c(nc.vector.tensor_tensor(st[:, 0, :], st[:, 0, :], sk, ALU.max))
                            dve_c(nc.vector.tensor_tensor(st[:, 2, :], sk, st[:, 0, :], ALU.subtract))
                        nc.vector.tensor_scalar(st[:, 1, :], st[:, 0, :], -1.0, None, ALU.mult).then_inc(neg_ready, 1)

                    def after(g):
                        dve.wait_ge(exp_ready, g + 1)
                        st = small[:, g % 2]
                        if masked is not None:
                            dve_c(nc.vector.tensor_tensor(st[:, 3, :], st[:, 3, :], st[:, 4, :], ALU.add))
                        dve_c(nc.vector.reciprocal(st[:, 5, :], st[:, 3, :]))
                        a, b = cols(g)
                        nc.vector.tensor_tensor(view(S, g), view(S, g), over_cols(st[:, 5, :], b - a),
                                                ALU.mult).then_inc(p_ready, 1)

                    def out(g):
                        evacuate_out("dve", dve, g, pv_done, o_used)

                    before(0)
                    before(1)
                    after(0)
                    for g in range(n):
                        if g + 2 < n:
                            before(g + 2)
                        if g + 1 < n:
                            after(g + 1)
                        out(g)

                @block.scalar
                def _(act):
                    act_c.eng = act

                    def exps(g):
                        act.wait_ge(neg_ready, g + 1)
                        st = small[:, g % 2]
                        for h in range(4):
                            act_c(nc.scalar.activation(view(S, g)[:, h, :], view(S, g)[:, h, :], ACT.Exp,
                                                       bias=st[:, 1, h:h + 1], accum_out=st[:, 3, h:h + 1]))
                        if masked is not None:
                            act_c(nc.scalar.activation(st[:, 4, :], st[:, 2, :], ACT.Exp))
                        act.sem_inc(exp_ready, 1)

                    def copy(g):
                        act.wait_ge(turned, g + 1)
                        if g >= 2:
                            act.wait_ge(pv_done, g - 1)
                        h0, h1 = groups[g][0], groups[g][-1] + 1
                        nc.scalar.activation(PT[:, g % 2, :].rearrange("p (a q) -> p a q", a=2)[:, h0:h1, :],
                                             ps[:, 4 + h0:4 + h1, :], ACT.Copy).then_inc(pt_ready, 1)

                    exps(0)
                    if n > 1:
                        exps(1)
                    copy(0)
                    for g in range(n):
                        if g + 2 < n:
                            exps(g + 2)
                        if g + 1 < n:
                            copy(g + 1)
                        evacuate_out("act", act, g, pv_done, o_used)

        def stage_window(l, q, kT, v):
            with ExitStack() as ph:
                def tmp(name, shape, dt=F32):
                    return ph.enter_context(nc.sbuf_tensor(name, shape, dt))

                vtok = tmp("v_rows", [P, NB, P])
                S = tmp("win_scores", [P, 2, 1024])
                PT = tmp("win_probsT", [P, 2, 1024])
                small = tmp("win_small", [P, 2, 8, 4])
                sinks = tmp("sinks", [P, NH])
                sink_rows = tmp("sink_rows", [64, 1])
                v_turned, v_copied, sinks_in, v_out = sem("v_turned"), sem("v_copied"), sem("sinks_in"), sem("v_out")
                with nc.Block() as block:
                    @block.sync
                    def _(sp):
                        sp.dma_start(sinks[:], io["attn_sinks"][l].unsqueeze(0).to_broadcast([P, NH])).then_inc(sinks_in, 16)
                        sp.dma_start(sink_rows[:], io["attn_sinks"][l].unsqueeze(1).to_broadcast([NH, 8]).unsqueeze(2))\
                            .then_inc(sinks_in, 16)
                        sp.wait_ge(sinks_in, 32)
                        sp.wait_ge(v_copied, 1)
                        sp.dma_start(io["win_v_prompt"][l, 0].rearrange("s k d -> s (k d)"), vtok[:, NB - 1, :])\
                            .then_inc(v_out, 16)
                        sp.wait_ge(v_out, 16)

                    @block.tensor
                    def _(pe):
                        for b in range(NB):
                            last = nc.tensor.transpose(ps[:, b // 4, P * (b % 4):P * (b % 4) + P],
                                                       v[:, P * b:P * b + P], ident[:])
                        last.then_inc(v_turned, 1)

                    @block.scalar
                    def _(act):
                        act.wait_ge(v_turned, 1)
                        nc.scalar.activation(vtok[:].rearrange("p (a b) d -> p a (b d)", a=2), ps[:, 0:2, :],
                                             ACT.Copy).then_inc(v_copied, 1)

                groups = [([1] if g < NKV else [0, 1]) for g in range(NB * NKV)]

                def score_mms(g, sv):
                    b, kv = divmod(g, NKV)
                    rows = slice(HD * kv, HD * kv + HD)
                    k0 = P * (b - 1) if b else 0
                    lo = 0 if b else P
                    for j in range(G):
                        last = nc.tensor.matmul(sv[:, j, lo:2 * P], q[rows, j, P * b:P * b + P],
                                                kT[rows, k0:P * (b + 1)], start=True, stop=True)
                    return last

                def pv_mms(pe, g, pt, o_used):
                    b, kv = divmod(g, NKV)
                    if b >= 2 and kv == 0:
                        pe.wait_ge(o_used, b - 1)
                    hs = groups[g]
                    for i, half in enumerate(hs):
                        last = nc.tensor.matmul(ps[HD * kv:HD * kv + HD, 6 + b % 2, :],
                                                vtok[:, b - 1 + half, HD * kv:HD * kv + HD],
                                                pt[:, half].rearrange("p h q -> p (h q)"), start=(i == 0),
                                                stop=(i == len(hs) - 1))
                    return last

                def evacuate_out(who, eng, g, pv_done, o_used):
                    b, kv = divmod(g, NKV)
                    if who == "act" and kv == 1:
                        eng.wait_ge(pv_done, g + 1)
                        nc.scalar.activation(Y[:, 0:G, P * b:P * b + P],
                                             ps[:, 6 + b % 2, :].rearrange("p (h q) -> p h q", h=G), ACT.Copy)\
                            .then_inc(o_used, 1)

                attention_blocks("win", groups, HD ** -0.5, (S, PT, small),
                                 (swa_mask, lambda g: sinks[:, G * (g % NKV):G * (g % NKV) + G]), lambda sp: None,
                                 score_mms, pv_mms, evacuate_out)

                kc, vc = S[:, 0, :], S[:, 1, :]
                kcT = PT[:, 0, :]
                sT = PT[:, 1, 0:64]
                prow = PT[0:64, 1, 128:128 + P + 1]
                prod = PT[:, 1, 320:352]
                pT = PT[:, 1, 384:448]
                dg = PT[0:64, 1, 512:576]
                t1 = PT[:, 1, 576:608]
                st = PT[0:64, 1, 640:648]
                kv_in, kc_turned, kc_copied, sT_ready, sT_copied, rows_ready, neg_s, exp_s, p_s, pT_ready, pT_copied, o_s, prod_s \
                    = (sem(f"ws_{n}") for n in ("kv_in", "kc_turned", "kc_copied", "sT", "sT_copied", "rows", "neg", "exp",
                                                "p", "pT", "pT_copied", "o", "prod"))
                with nc.Block() as block:
                    @block.sync
                    def _(sp):
                        sp.dma_start(kc.rearrange("s (b c) -> s b c", b=NS),
                                     io["cache_win_k"][l].rearrange("b s k d -> s b (k d)")).then_inc(kv_in, 16)
                        sp.dma_start(vc.rearrange("s (b c) -> s b c", b=NS),
                                     io["cache_win_v"][l].rearrange("b s k d -> s b (k d)")).then_inc(kv_in, 16)

                    @block.tensor
                    def _(pe):
                        pe.wait_ge(kv_in, 32)
                        for b in range(NS):
                            last = nc.tensor.transpose(ps[:, b // 4, P * (b % 4):P * (b % 4) + P], kc[:, P * b:P * b + P],
                                                       ident[:])
                        last.then_inc(kc_turned, 1)
                        pe.wait_ge(kc_copied, 1)
                        pe.wait_ge(prod_s, 1)
                        s_out = ps[:, 2:4, 0:32].rearrange("p k (j b) -> p k j b", j=G)
                        for b in range(NS):
                            for kv in range(NKV):
                                r = slice(HD * kv, HD * kv + HD)
                                last = nc.tensor.matmul(s_out[:, kv, :, b], kcT[r, P * b:P * b + P], q[r, :, SEQ + b],
                                                        start=True, stop=True)
                        last.then_inc(sT_ready, 1)
                        pe.wait_ge(sT_copied, 1)
                        nc.tensor.transpose(ps[0:64, 4, 0:P], sT, ident[:])
                        for kv in range(NKV):
                            r = slice(HD * kv, HD * kv + HD)
                            last = nc.tensor.matmul(ps[32 * kv:32 * kv + 32, 5 + kv, 0:1], prod[r, :], ones[r, 0:1],
                                                    start=True, stop=True)
                        last.then_inc(rows_ready, 1)
                        pe.wait_ge(p_s, 1)
                        nc.tensor.transpose(ps[:, 7, 0:64], prow[:, 0:P], ident[0:64, 0:64])
                        nc.tensor.matmul(ps[:, 0, 0:64], ones[0:64, :], dg, start=True, stop=True).then_inc(pT_ready, 1)
                        pe.wait_ge(pT_copied, 1)
                        pTv = pT.rearrange("p (k j b) -> p k j b", k=NKV, j=G)
                        o_out = ps[:, 1, 0:32].rearrange("p (j b) -> p j b", j=G)
                        for b in range(NS):
                            for kv in range(NKV):
                                last = nc.tensor.matmul(o_out[HD * kv:HD * kv + HD, :, b],
                                                        vc[:, P * b + HD * kv:P * b + HD * kv + HD], pTv[:, kv, :, b],
                                                        start=True, stop=True)
                        last.then_inc(o_s, 1)

                    @block.scalar
                    def _(act):
                        act_c.eng = act
                        act.wait_ge(kc_turned, 1)
                        nc.scalar.activation(kcT.rearrange("p (a c) -> p a c", a=2), ps[:, 0:2, :], ACT.Copy)\
                            .then_inc(kc_copied, 1)
                        act.wait_ge(neg_s, 1)
                        act_c(nc.scalar.activation(prow, prow, ACT.Exp, bias=st[:, 1:2], accum_out=st[:, 3:4]))
                        nc.scalar.activation(st[:, 4:5], st[:, 2:3], ACT.Exp).then_inc(exp_s, 1)

                    @block.vector
                    def _(dve):
                        dve_c.eng = dve
                        nc.vector.tensor_tensor(prod.rearrange("p (j b) -> p j b", j=G), q[:, :, SEQ:T],
                                                over_heads(kT[:, SEQ:T], G), ALU.mult).then_inc(prod_s, 1)
                        dve.wait_ge(sT_ready, 1)
                        nc.vector.tensor_copy(sT.rearrange("p (k c) -> p k c", k=NKV), ps[:, 2:4, 0:32]).then_inc(sT_copied, 1)
                        dve.wait_ge(rows_ready, 1)
                        sc = HD ** -0.5
                        dve_c(nc.vector.tensor_scalar(prow[:, 0:P], ps[0:64, 4, 0:P], sc, None, ALU.mult))
                        for kv in range(NKV):
                            r = slice(32 * kv, 32 * kv + 32)
                            dve_c(nc.vector.tensor_scalar(prow[r, P:P + 1], ps[r, 5 + kv, 0:1], sc, None, ALU.mult))
                        dve_c(nc.vector.tensor_reduce(st[:, 0:1], prow, AX.X, ALU.max))
                        dve_c(nc.vector.tensor_tensor(st[:, 0:1], st[:, 0:1], sink_rows[:], ALU.max))
                        dve_c(nc.vector.tensor_tensor(st[:, 2:3], sink_rows[:], st[:, 0:1], ALU.subtract))
                        nc.vector.tensor_scalar(st[:, 1:2], st[:, 0:1], -1.0, None, ALU.mult).then_inc(neg_s, 1)
                        dve.wait_ge(exp_s, 1)
                        dve_c(nc.vector.tensor_tensor(st[:, 5:6], st[:, 3:4], st[:, 4:5], ALU.add))
                        dve_c(nc.vector.reciprocal(st[:, 6:7], st[:, 5:6]))
                        dve_c(nc.vector.tensor_scalar(prow, prow, st[:, 6:7], None, ALU.mult))
                        nc.vector.tensor_scalar(dg, ident[0:64, 0:64], prow[:, P:P + 1], None, ALU.mult).then_inc(p_s, 1)
                        dve.wait_ge(pT_ready, 1)
                        nc.vector.tensor_copy(pT, ps[:, 7, 0:64]).then_inc(pT_copied, 1)
                        for kv in range(NKV):
                            r = slice(HD * kv, HD * kv + HD)
                            dve_c(nc.vector.tensor_tensor(t1[r, :].rearrange("p (j b) -> p j b", j=G),
                                                          ps[r, 0, 32 * kv:32 * kv + 32].rearrange("p (j b) -> p j b", j=G),
                                                          over_heads(v[r, SEQ:T], G), ALU.mult))
                        dve.wait_ge(o_s, 1)
                        dve_c(nc.vector.tensor_tensor(Y[:, 0:G, SEQ:T], ps[:, 1, 0:32].rearrange("p (j b) -> p j b", j=G),
                                                      t1.rearrange("p (j b) -> p j b", j=G), ALU.add))

        def stage_hgrn(l):
            with ExitStack() as ph:
                def tmp(name, shape, dt=F32):
                    return ph.enter_context(nc.sbuf_tensor(name, shape, dt))

                Q, K, Gt, B = (tmp(f"hg_{n}", [P, T]) for n in ("q", "k", "g", "b"))
                Xa = tmp("hg_x", [P, 2, 1024])
                X = [Xa[:, 0, :], Xa[:, 1, :]]
                E = tmp("hg_s", [P, 1024])
                att = tmp("hg_att", [P, 1024])
                vtok, ktok = tmp("hg_vrows", [P, 1024]), tmp("hg_krows", [P, 1024])
                bl = tmp("hg_blast", [P, NB])
                fs, sv, sq8 = (tmp(f"hg_{n}", [P, NS]) for n in ("fs", "sv", "sq8"))
                vrow = tmp("hg_vrow", [NS, P])
                s = {n: sem(f"hg_{n}") for n in (
                    "out", "sp", "k", "lnf", "e", "exp", "x", "lvl", "lvl_used", "vt", "vt_copied", "eb", "xs", "kh", "kt",
                    "kt_copied", "qe", "ds", "state", "o", "osq", "mean", "root", "st_in", "vs", "vdiag", "vb", "snew", "os",
                    "st_out", "normed")}
                BA, BB, BC = 3, 5, 7
                NL = LEVELS + 1

                def pair(b):
                    return ps[:, b:b + 2, :]

                def two(t):
                    return t.rearrange("p (a c) -> p a c", a=2)

                def chunks(t):
                    return t.rearrange("p (c t) -> p c t", t=P)

                def in_pair(b, c, m=P):
                    return ps[0:m, b + c // 4, P * (c % 4):P * (c % 4) + P]

                def level_bank(lv):
                    return BA if lv % 2 else BB

                def slabs(r):
                    return [S_HGRN + 4 * r + i for i in range(4)] if r < RH else []

                with nc.Block() as block:
                    @block.sync
                    def _(sp):
                        load_slabs(sp, l, 6)
                        for r in range(RH):
                            if r:
                                sp.wait_ge(s["os"], r)
                            sp.dma_start(E[:].rearrange("k (b v) -> k b v", b=NS),
                                         io["state_hgrn"][l, :, r].rearrange("b k v -> k b v")).then_inc(s["st_in"], 16)
                            load_slabs(sp, l, min(4 * (r + 2) + 2, N_HGRN + 2))
                            sp.wait_ge(s["state"], r + 1)
                            sp.dma_start(io["hgrn_prompt"][l, 0, r], X[0][:, P * (NB - 1):P * NB]).then_inc(s["st_out"], 16)
                            sp.wait_ge(s["snew"], r + 1)
                            sp.dma_start(io["hgrn_sample"][l, :, r].rearrange("b k v -> k b v"),
                                         E[:].rearrange("k (b v) -> k b v", b=NS)).then_inc(s["st_out"], 16)
                            sp.wait_ge(s["st_out"], 32 * (r + 1))

                    @block.gpsimd
                    def _(pool):
                        split_lo(pool, N_HGRN + 2)

                    @block.tensor
                    def _(pe):
                        def level(r, lv):
                            i = NL * r + lv
                            if lv == 0:
                                pe.wait_ge(s["k"], r + 1)
                            else:
                                pe.wait_ge(s["x"], LEVELS * r + lv)
                            if lv == 1:
                                pe.wait_ge(s["vt_copied"], r + 1)
                            if lv >= 2:
                                pe.wait_ge(s["lvl_used"], i - 1)
                            a, b2 = (K[:], Q[:]) if lv == 0 else (X[lv % 2], X[lv % 2])
                            for c in range(NB):
                                last = nc.tensor.matmul(in_pair(level_bank(lv), c), a[:, P * c:P * c + P],
                                                        b2[:, P * c:P * c + P], start=True, stop=True)
                            last.then_inc(s["lvl"], 1)

                        def ahead(r, i):
                            if r + 1 < RH:
                                pe.wait_ge(s["out"], 4 * (r + 1) + i)
                                project(pe, slabs(r + 1)[i], 0)

                        for i, n in enumerate(slabs(0)):
                            if i >= 2:
                                pe.wait_ge(s["out"], i - 1)
                            project(pe, n, 3 * (i % 2))
                        for r in range(RH):
                            pe.wait_ge(s["out"], 4 * (r + 1))
                            if r:
                                pe.wait_ge(s["normed"], r)
                            for c in range(NB):
                                last = nc.tensor.transpose(in_pair(BA, c), Y[:, 2, P * c:P * c + P], ident[:])
                            last.then_inc(s["vt"], 1)
                            level(r, 0)
                            ahead(r, 0)
                            level(r, 1)
                            level(r, 2)
                            ahead(r, 1)
                            level(r, 3)
                            level(r, 4)
                            ahead(r, 2)
                            level(r, 5)
                            level(r, 6)
                            level(r, 7)
                            ahead(r, 3)
                            pe.wait_ge(s["kh"], r + 1)
                            pe.wait_ge(s["lvl_used"], NL * (r + 1))
                            for c in range(NB):
                                last = nc.tensor.transpose(in_pair(BB, c), X[0][:, P * c:P * c + P], ident[:])
                            last.then_inc(s["kt"], 1)
                            nc.tensor.transpose(ps[0:NS, BC, 0:P], sv[:], ident[:]).then_inc(s["vs"], 1)
                            pe.wait_ge(s["kt_copied"], r + 1)
                            for c in range(NB):
                                cc = slice(P * c, P * c + P)
                                last = nc.tensor.matmul(in_pair(BA, c), ktok[:, cc], vtok[:, cc], start=True, stop=True)
                            last.then_inc(s["ds"], 1)
                            pe.wait_ge(s["qe"], r + 1)
                            pe.wait_ge(s["state"], r + 1)
                            for c in range(NB):
                                cc = slice(P * c, P * c + P)
                                last = nc.tensor.matmul(in_pair(BB, c), vtok[:, cc], att[:, cc], start=True, stop=(c == 0))
                                if c:
                                    last = nc.tensor.matmul(in_pair(BB, c), X[0][:, P * (c - 1):P * c], Q[:, cc],
                                                            start=False, stop=True)
                            last.then_inc(s["o"], 1)
                            pe.wait_ge(s["vdiag"], r + 1)
                            for h in range(2):
                                last = nc.tensor.matmul(ps[:, BA + h, :], ones[0:NS, :], ktok[0:NS, 512 * h:512 * h + 512],
                                                        start=True, stop=True)
                            last.then_inc(s["vb"], 1)
                            pe.wait_ge(s["snew"], r + 1)
                            for b in range(NS):
                                last = nc.tensor.matmul(ps[:, BC, 256 + b:257 + b], E[:, P * b:P * b + P],
                                                        Q[:, SEQ + b:SEQ + b + 1], start=True, stop=True)
                            last.then_inc(s["os"], 1)
                            pe.wait_ge(s["osq"], r + 1)
                            for h in range(2):
                                nc.tensor.matmul(ps[:, BA + h, :], ones[:], att[:, 512 * h:512 * h + 512], start=True, stop=True)
                            nc.tensor.matmul(ps[:, BC, 272:272 + NS], ones[:], sq8[:], start=True, stop=True)\
                                .then_inc(s["mean"], 1)

                    @block.scalar
                    def _(act):
                        act_c.eng = act

                        def exp_level(r, lv):
                            act.wait_ge(s["e"], LEVELS * r + lv)
                            nc.scalar.activation(X[lv % 2], X[lv % 2], ACT.Exp).then_inc(s["exp"], 1)

                        split_hi(act, 6)
                        for r in range(RH):
                            nx = min(4 * (r + 1), N_HGRN - 4)
                            act.wait_ge(s["out"], 4 * (r + 1))
                            if r:
                                act.wait_ge(s["normed"], r)
                            act_c(nc.scalar.activation(Q[:], Y[:, 0, :], ACT.Silu))
                            act_c(nc.scalar.activation(Gt[:], Y[:, 3, :], ACT.Silu))
                            act_c(nc.scalar.activation(K[:], Y[:, 1, :], ACT.Sigmoid, scale=-1.0))
                            nc.scalar.activation(B[:], Y[:, 1, :], ACT.Sigmoid).then_inc(s["sp"], 1)
                            act.wait_ge(s["vt"], r + 1)
                            nc.scalar.activation(two(vtok[:]), pair(BA), ACT.Copy).then_inc(s["vt_copied"], 1)
                            act.wait_ge(s["k"], r + 1)
                            nc.scalar.activation(B[:], B[:], ACT.Ln, bias=lbt[:, r:r + 1],
                                                 scale=oml[:, r:r + 1]).then_inc(s["lnf"], 1)
                            exp_level(r, 1)
                            exp_level(r, 2)
                            split_hi(act, nx + 3)
                            exp_level(r, 3)
                            exp_level(r, 4)
                            split_hi(act, nx + 4)
                            exp_level(r, 5)
                            exp_level(r, 6)
                            split_hi(act, nx + 5)
                            exp_level(r, 7)
                            act.wait_ge(s["eb"], 2 * r + 1)
                            nc.scalar.activation(X[0], X[0], ACT.Exp).then_inc(s["xs"], 1)
                            act.wait_ge(s["eb"], 2 * r + 2)
                            act_c(nc.scalar.activation(bl[:], chunks(B[:, 0:SEQ])[:, :, P - 1], ACT.Exp))
                            nc.scalar.activation(X[1], B[:, 0:SEQ], ACT.Exp).then_inc(s["xs"], 1)
                            split_hi(act, nx + 6)
                            act.wait_ge(s["kt"], r + 1)
                            nc.scalar.activation(two(ktok[:]), pair(BB), ACT.Copy).then_inc(s["kt_copied"], 1)
                            act.wait_ge(s["o"], r + 1)
                            act_c(nc.scalar.activation(two(att[:]), pair(BB), ACT.Square))
                            act.wait_ge(s["os"], r + 1)
                            nc.scalar.activation(sq8[:], ps[:, BC, 256:256 + NS], ACT.Square).then_inc(s["osq"], 1)
                            act.wait_ge(s["mean"], r + 1)
                            act_c(nc.scalar.activation(two(X[1]), pair(BA), ACT.Sqrt, bias=epst[:], scale=1.0 / P))
                            nc.scalar.activation(sq8[:], ps[:, BC, 272:272 + NS], ACT.Sqrt, bias=epst[:],
                                                 scale=1.0 / P).then_inc(s["root"], 1)

                    @block.vector
                    def _(dve):
                        dve_c.eng = dve

                        def evacuate(n, bank):
                            dve.wait_ge(w_used, n + 1)
                            nc.vector.tensor_tensor(tokens3(Y[:, n % 4, :]), ps[:, bank:bank + 3, 0:CH], tokens3(rs[:]),
                                                    ALU.mult).then_inc(s["out"], 1)

                        def ahead(r, i):
                            if r + 1 < RH:
                                evacuate(slabs(r + 1)[i], 0)

                        def halves(t, lv, k):
                            hf = 1 << (lv - 1)
                            return t.rearrange("p (n h) -> p n h", h=2 * hf)[:, :, hf * k:hf * k + hf]

                        def distances(r, lv):
                            hf = 1 << (lv - 1)
                            bv = B[:, 0:SEQ]
                            mid = bv.rearrange("p (n h) -> p n h", h=2 * hf)[:, :, hf - 1:hf].to_broadcast(
                                [P, SEQ // (2 * hf), hf])
                            x = X[lv % 2]
                            dve_c(nc.vector.tensor_tensor(halves(x, lv, 0), mid, halves(bv, lv, 0), ALU.subtract))
                            nc.vector.tensor_tensor(halves(x, lv, 1), halves(bv, lv, 1), mid, ALU.subtract).then_inc(s["e"], 1)

                        def weigh(r, lv):
                            dve.wait_ge(s["exp"], LEVELS * r + lv)
                            x = X[lv % 2]
                            dve_c(nc.vector.tensor_tensor(halves(x, lv, 0), halves(x, lv, 0), halves(K[:, 0:SEQ], lv, 0), ALU.mult))
                            nc.vector.tensor_tensor(halves(x, lv, 1), halves(x, lv, 1), halves(Q[:, 0:SEQ], lv, 1), ALU.mult)\
                                .then_inc(s["x"], 1)

                        def take(r, lv):
                            i = NL * r + lv
                            dve.wait_ge(s["lvl"], i + 1)
                            for h in range(2):
                                dst = chunks(att[:, 512 * h:512 * h + 512])
                                sc = chunks(ps[:, level_bank(lv) + h, :])
                                if lv == 0:
                                    last = nc.vector.tensor_tensor(dst, sc, over_heads(ident[:], 4), ALU.mult)
                                else:
                                    last = nc.vector.copy_predicated(dst, over_heads(lvl_mask[:, lv - 1, :], 4), sc)
                                if h == 0:
                                    dve_c(last)
                            last.then_inc(s["lvl_used"], 1)
                            dve.wait_ge(s["lvl_used"], i + 1)

                        for i, n in enumerate(slabs(0)):
                            evacuate(n, 3 * (i % 2))
                        for r in range(RH):
                            dve.wait_ge(s["out"], 4 * (r + 1))
                            dve_c(nc.vector.tensor_copy(sv[:], Y[:, 2, SEQ:T]))
                            dve.wait_ge(s["sp"], r + 1)
                            dve_c(nc.vector.tensor_scalar(fs[:], B[:, SEQ:T], oml[:, r:r + 1], lbt[:, r:r + 1],
                                                          ALU.mult, ALU.add))
                            nc.vector.tensor_scalar(K[:], K[:], oml[:, r:r + 1], None, ALU.mult).then_inc(s["k"], 1)
                            dve.wait_ge(s["k"], r + 1)
                            dve.wait_ge(s["lnf"], r + 1)
                            dve_c(nc.vector.tensor_tensor_scan(B[:, 0:SEQ], restart[:], B[:, 0:SEQ], 0.0, ALU.mult, ALU.add))
                            distances(r, 1)
                            if r:
                                dve.wait_ge(s["st_out"], 32 * r)
                            distances(r, 2)
                            take(r, 0)
                            weigh(r, 1)
                            weigh(r, 2)
                            ahead(r, 0)
                            take(r, 1)
                            distances(r, 3)
                            take(r, 2)
                            distances(r, 4)
                            weigh(r, 3)
                            weigh(r, 4)
                            ahead(r, 1)
                            take(r, 3)
                            distances(r, 5)
                            take(r, 4)
                            distances(r, 6)
                            weigh(r, 5)
                            weigh(r, 6)
                            ahead(r, 2)
                            take(r, 5)
                            distances(r, 7)
                            weigh(r, 7)
                            take(r, 6)
                            b3 = chunks(B[:, 0:SEQ])
                            nc.vector.tensor_tensor(chunks(X[0]), b3[:, :, P - 1:P].to_broadcast([P, NB, P]), b3, ALU.subtract)\
                                .then_inc(s["eb"], 1)
                            take(r, 7)
                            dve.sem_inc(s["eb"], 1)
                            dve.wait_ge(s["xs"], 2 * r + 1)
                            nc.vector.tensor_tensor(X[0], X[0], K[:, 0:SEQ], ALU.mult).then_inc(s["kh"], 1)
                            dve.wait_ge(s["xs"], 2 * r + 2)
                            nc.vector.tensor_tensor(Q[:, 0:SEQ], Q[:, 0:SEQ], X[1], ALU.mult).then_inc(s["qe"], 1)
                            dve.wait_ge(s["qe"], r + 1)
                            ahead(r, 3)
                            dve.wait_ge(s["vs"], r + 1)
                            dve_c(nc.vector.tensor_copy(vrow[:], ps[0:NS, BC, 0:P]))
                            dve.wait_ge(s["ds"], r + 1)
                            for c in range(NB):
                                new = X[0][:, P * c:P * c + P]
                                if c == 0:
                                    last = nc.vector.tensor_copy(new, in_pair(BA, c))
                                else:
                                    last = nc.vector.scalar_tensor_tensor(new, X[0][:, P * (c - 1):P * c], bl[:, c:c + 1],
                                                                          in_pair(BA, c), ALU.mult, ALU.add)
                                if c < NB - 1:
                                    dve_c(last)
                            last.then_inc(s["state"], 1)
                            nc.vector.tensor_tensor(chunks(ktok[0:NS, :]), over_heads(vrow[:], NS),
                                                    over_cols(ident[0:NS, 0:NS], P), ALU.mult).then_inc(s["vdiag"], 1)
                            dve.wait_ge(s["st_in"], 16 * (r + 1))
                            dve_c(nc.vector.tensor_tensor(chunks(E[:]), chunks(E[:]), over_cols(fs[:], P), ALU.mult))
                            dve.wait_ge(s["vb"], r + 1)
                            for h in range(2):
                                dve_c(nc.vector.tensor_tensor(chunks(X[1][:, 512 * h:512 * h + 512]), chunks(ps[:, BA + h, :]),
                                                              over_cols(K[:, SEQ + 4 * h:SEQ + 4 * h + 4], P), ALU.mult))
                            nc.vector.tensor_tensor(E[:], E[:], X[1], ALU.add).then_inc(s["snew"], 1)
                            gn = gT[:, G_HGRN + r:G_HGRN + r + 1]
                            y = Y[:, 4 + r, :]
                            dve.wait_ge(s["root"], r + 1)
                            dve_c(nc.vector.scalar_tensor_tensor(two(y[:, 0:SEQ]), pair(BB), gn, two(Gt[:, 0:SEQ]),
                                                                 ALU.mult, ALU.mult))
                            dve_c(nc.vector.reciprocal(X[1], X[1]))
                            dve_c(nc.vector.reciprocal(sq8[:], sq8[:]))
                            dve_c(nc.vector.tensor_tensor(y[:, 0:SEQ], y[:, 0:SEQ], X[1], ALU.mult))
                            dve_c(nc.vector.scalar_tensor_tensor(y[:, SEQ:T], ps[:, BC, 256:256 + NS], gn, Gt[:, SEQ:T],
                                                                 ALU.mult, ALU.mult))
                            nc.vector.tensor_tensor(y[:, SEQ:T], y[:, SEQ:T], sq8[:], ALU.mult).then_inc(s["normed"], 1)
                            dve.wait_ge(s["normed"], r + 1)
        def stage_project(name, l, n0, count, split_first, scaled):
            out, hi_ready, lo_ready = sem(f"{name}_out"), sem(f"{name}_hi"), sem(f"{name}_lo")
            with nc.Block() as block:
                @block.sync
                def _(sp):
                    load_slabs(sp, l, n0 + count + 2)

                @block.gpsimd
                def _(pool):
                    split_lo(pool, n0 + count)

                @block.tensor
                def _(pe):
                    if split_first:
                        pe.wait_ge(lo_ready, KT)
                    for i in range(count):
                        if i >= 2:
                            pe.wait_ge(out, i - 1)
                        project(pe, n0 + i, 3 * (i % 2))

                @block.scalar
                def _(act):
                    if split_first:
                        for k in range(KT):
                            nc.scalar.activation(hh[:, k, :], Y[:, k, :], ACT.Copy).then_inc(hi_ready, 1)
                    for i in range(count):
                        split_hi(act, min(n0 + i + 2, n0 + count))
                        if not scaled:
                            act.wait_ge(w_used, n0 + i + 1)
                            nc.scalar.activation(tokens3(Y[:, i, :]), ps[:, 3 * (i % 2):3 * (i % 2) + 3, 0:CH],
                                                 ACT.Copy).then_inc(out, 1)

                @block.vector
                def _(dve):
                    if split_first:
                        for k in range(KT):
                            dve.wait_ge(hi_ready, k + 1)
                            nc.vector.tensor_tensor(hl[:, k, :], Y[:, k, :], hh[:, k, :].bitcast(F32), ALU.subtract)\
                                .then_inc(lo_ready, 1)
                    if scaled:
                        for i in range(count):
                            dve.wait_ge(w_used, n0 + i + 1)
                            nc.vector.tensor_tensor(tokens3(Y[:, i, :]), ps[:, 3 * (i % 2):3 * (i % 2) + 3, 0:CH],
                                                    tokens3(rs[:]), ALU.mult).then_inc(out, 1)

        def stage_memory(l, mkT, mv):
            with ExitStack() as ph:
                def tmp(name, shape, dt=F32):
                    return ph.enter_context(nc.sbuf_tensor(name, shape, dt))

                mem = tmp("mem_rows", [P, 2, D])
                mh, ml = tmp("mem_hi", [P, KT, NMEM], F32R), tmp("mem_lo", [P, KT, NMEM], F32R)
                mstat = tmp("mem_stat", [P, 3, 2])
                mem_in, turned, m_hi, m_lo, m_sq, m_root, m_rs, kv_copied, k_turned, mem_out, k_acc, v_acc = (
                    sem(f"mem_{n}") for n in ("in", "turned", "hi", "lo", "sq", "root", "rs", "kv_copied", "k_turned", "out",
                                              "k", "v"))
                with nc.Block() as block:
                    @block.sync
                    def _(sp):
                        sp.dma_start(mem[:], io["mem_prompt"][0].rearrange("(a p) f -> p a f", p=P)).then_inc(mem_in, 16)
                        load_slabs(sp, l, S_XQ + 2)
                        sp.wait_ge(kv_copied, 2)
                        sp.dma_start(io["mem_k_prompt"][l, 0].rearrange("(a p) h d -> p a (h d)", p=P), mem[:]).then_inc(mem_out, 16)
                        sp.wait_ge(kv_copied, 4)
                        sp.dma_start(io["mem_v_prompt"][l, 0].rearrange("(a p) h d -> p a (h d)", p=P), mv[:]).then_inc(mem_out, 16)
                        sp.wait_ge(mem_out, 32)

                    @block.gpsimd
                    def _(pool):
                        split_lo(pool, S_XQ)

                    @block.tensor
                    def _(pe):
                        pe.wait_ge(mem_in, 16)
                        for a in range(2):
                            for k in range(KT):
                                last = nc.tensor.transpose(ps[:, k // 2, 256 * (k % 2) + P * a:256 * (k % 2) + P * a + P],
                                                           mem[:, a, P * k:P * k + P], ident[:])
                        last.then_inc(turned, 1)
                        pe.wait_ge(m_lo, KT)
                        for n in range(S_MEM, S_XQ):
                            which, k = divmod(n - S_MEM, KT)
                            if which == 0 and k == 0:
                                pe.wait_ge(m_rs, 1)
                            pe.wait_ge(lo_done, n + 1)
                            for a in range(2):
                                for h in range(2):
                                    bank = 4 - 4 * which + 2 * a + h
                                    out = ps[:, bank, :]
                                    sl = slice(512 * h, 512 * h + 512)
                                    x1, x2 = mh[:, k, P * a:P * a + P], ml[:, k, P * a:P * a + P]
                                    w1, w2 = w_hi[:, n % 2, sl], w_lo[:, n % 2, sl]
                                    nc.tensor.matmul(out, x1, w1, start=(k == 0), stop=False)
                                    nc.tensor.matmul(out, x1, w2, start=False, stop=False)
                                    last = nc.tensor.matmul(out, x2, w1, start=False, stop=(k == KT - 1))
                            last.then_inc(w_used, 1)
                        pe.wait_ge(kv_copied, 2)
                        for k in range(KT):
                            for a in range(2):
                                last = nc.tensor.transpose(ps[:, 4 + k // 2, 256 * (k % 2) + P * a:256 * (k % 2) + P * a + P],
                                                           mem[:, a, P * k:P * k + P], ident[:])
                        last.then_inc(k_turned, 1)

                    @block.scalar
                    def _(act):
                        act_c.eng = act
                        act.wait_ge(mem_in, 16)
                        for a in range(2):
                            act_c(nc.scalar.activation(mv[:, a, :], mem[:, a, :], ACT.Square, accum_out=mstat[:, 0, a:a + 1]))
                        nc.scalar.activation(mstat[:, 1, :], mstat[:, 0, :], ACT.Sqrt, bias=epst[:], scale=1.0 / D)\
                            .then_inc(m_root, 1)
                        act.wait_ge(turned, 1)
                        for k in range(KT):
                            nc.scalar.activation(mh[:, k, :], ps[:, k // 2, 256 * (k % 2):256 * (k % 2) + 256], ACT.Copy,
                                                 scale=gT[:, G_MEM + k:G_MEM + k + 1]).then_inc(m_hi, 1)
                        for which in range(2):
                            for k in range(KT):
                                n = S_MEM + KT * which + k
                                split_hi(act, min(n + 2, S_XQ))
                            act.wait_ge(w_used, S_MEM + KT * which + KT)
                            act.wait_ge(m_rs, 1)
                            dst = mv if which else mem
                            for a in range(2):
                                b = 4 - 4 * which + 2 * a
                                nc.scalar.activation(dst[:, a, :].rearrange("p (h c) -> p h c", h=2), ps[:, b:b + 2, :], ACT.Copy,
                                                     scale=mstat[:, 2, a:a + 1]).then_inc(kv_copied, 1)
                        act.wait_ge(k_turned, 1)
                        nc.scalar.activation(mkT[:].rearrange("p (b k) t -> p b (k t)", k=2), ps[:, 4:8, :], ACT.Copy)

                    @block.vector
                    def _(dve):
                        dve_c.eng = dve
                        dve.wait_ge(m_root, 1)
                        dve_c(nc.vector.reciprocal(mstat[:, 2, :], mstat[:, 1, :]))
                        for k in range(KT):
                            dve.wait_ge(m_hi, (k | 1) + 1)
                            nc.vector.scalar_tensor_tensor(ml[:, k, :], ps[:, k // 2, 256 * (k % 2):256 * (k % 2) + 256],
                                                           gT[:, G_MEM + k:G_MEM + k + 1], mh[:, k, :].bitcast(F32),
                                                           ALU.mult, ALU.subtract).then_inc(m_lo, 1)
                        dve.wait_ge(m_lo, KT)
                        dve.sem_inc(m_rs, 1)

        def stage_cross(l, mkT, mv):
            with ExitStack() as ph:
                S = ph.enter_context(nc.sbuf_tensor("x_scores", [P, 2, 1024], F32))
                PT = ph.enter_context(nc.sbuf_tensor("x_probsT", [P, 2, 1024], F32))
                small = ph.enter_context(nc.sbuf_tensor("x_small", [P, 2, 8, 4], F32))
                x_hi = sem("x_hi")

                def score_mms(g, sv):
                    for h in range(XH):
                        for d in range(2):
                            last = nc.tensor.matmul(sv[:, h, :], Y[:, 2 * h + d, P * g:P * g + P], mkT[:, 2 * h + d, :],
                                                    start=(d == 0), stop=(d == 1))
                    return last

                def pv_mms(pe, g, pt, o_used):
                    if g:
                        pe.wait_ge(o_used, g)
                    for k in range(KT):
                        for half in range(2):
                            last = nc.tensor.matmul(ps[:, 6 + k // 4, P * (k % 4):P * (k % 4) + P],
                                                    mv[:, half, P * k:P * k + P], pt[:, half, k // 2, :],
                                                    start=(half == 0), stop=(half == 1))
                    return last

                def evacuate_out(who, eng, g, pv_done, o_used):
                    src = ps[:, 6:8, :].rearrange("p b (k q) -> p b k q", k=4)
                    hi = hh[:, :, P * g:P * g + P].rearrange("p (b k) q -> p b k q", b=2)
                    lo = hl[:, :, P * g:P * g + P].rearrange("p (b k) q -> p b k q", b=2)
                    if who == "act":
                        eng.wait_ge(pv_done, g + 1)
                        for b in range(2):
                            nc.scalar.activation(hi[:, b], src[:, b], ACT.Copy).then_inc(x_hi, 1)
                    else:
                        eng.wait_ge(x_hi, 2 * g + 2)
                        dve_c(nc.vector.tensor_tensor(lo[:, 0], src[:, 0], hi[:, 0].bitcast(F32), ALU.subtract))
                        nc.vector.tensor_tensor(lo[:, 1], src[:, 1], hi[:, 1].bitcast(F32), ALU.subtract).then_inc(o_used, 1)

                attention_blocks("x", [[0, 1]] * NB, 256 ** -0.5, (S, PT, small), None, lambda sp: None,
                                 score_mms, pv_mms, evacuate_out)

        def stage_cross_samples(l):
            RING = 3
            with ExitStack() as ph:
                def tmp(name, shape, dt=F32):
                    return ph.enter_context(nc.sbuf_tensor(name, shape, dt))

                kv = tmp("xs_cache", [P, RING, 2, D])
                cT_ = tmp("xs_keysT", [P, 2, KT, NMEM])
                qs = tmp("xs_q", [P, KT, NS])
                sT = tmp("xs_scoresT", [P, 2, 32])
                rows = tmp("xs_rows", [32, NMEM])
                pT = tmp("xs_probsT", [P, 2, 32])
                st = tmp("xs_stat", [32, 4])
                kv_in = [sem(f"xs_in{i}") for i in range(RING)]
                k_copied = [sem("xs_copied0"), sem("xs_copied1")]
                q_ready = sem("xs_q_ready")
                k_turned, s_done, sT_ready, rows_ready, neg_r, exp_r, p_r, pT_ready, pT_copied, v_done, hi_r = (
                    sem(f"xs_{n}") for n in ("turned", "scored", "sT", "rows", "neg", "exp", "p", "pT", "pT_copied",
                                             "v_done", "hi"))
                with nc.Block() as block:
                    @block.sync
                    def _(sp):
                        for i in range(2 * NS):
                            which, b = divmod(i, NS)
                            last = i - RING
                            if 0 <= last < NS:
                                sp.wait_ge(k_turned, 2 * (last + 1))
                            elif last >= NS:
                                sp.wait_ge(v_done, last + 1 - NS)
                            src = io[("cache_mem_k", "cache_mem_v")[which]][l, b].rearrange("(a p) h d -> p a (h d)", p=P)
                            sp.dma_start(kv[:, i % RING], src).then_inc(kv_in[i % RING], 16)

                    def score(pe, b):
                        pe.wait_ge(q_ready, 1)
                        for hf in range(2):
                            pe.wait_ge(k_copied[hf], b + 1)
                        for a in range(2):
                            for h in range(XH):
                                for d in range(2):
                                    last = nc.tensor.matmul(ps[:, 4, 32 * a + NS * h + b:32 * a + NS * h + b + 1],
                                                            cT_[:, b % 2, 2 * h + d, P * a:P * a + P], qs[:, 2 * h + d, b:b + 1],
                                                            start=(d == 0), stop=(d == 1))
                        last.then_inc(s_done, 1)

                    @block.tensor
                    def _(pe):
                        for b in range(NS):
                            pe.wait_ge(kv_in[b % RING], 16 * (b // RING + 1))
                            for hf in range(2):
                                if b:
                                    pe.wait_ge(k_copied[hf], b)
                                for k in range(4 * hf, 4 * hf + 4):
                                    for a in range(2):
                                        last = nc.tensor.transpose(
                                            ps[:, k // 2, 256 * (k % 2) + P * a:256 * (k % 2) + P * a + P],
                                            kv[:, b % RING, a, P * k:P * k + P], ident[:])
                                last.then_inc(k_turned, 1)
                            if b:
                                score(pe, b - 1)
                        score(pe, NS - 1)
                        pe.wait_ge(sT_ready, 1)
                        for a in range(2):
                            last = nc.tensor.transpose(ps[0:32, 5, P * a:P * a + P], sT[:, a, :], ident[:])
                        last.then_inc(rows_ready, 1)
                        pe.wait_ge(p_r, 1)
                        for a in range(2):
                            last = nc.tensor.transpose(ps[:, 6, 32 * a:32 * a + 32], rows[:, P * a:P * a + P], ident[0:32, 0:32])
                        last.then_inc(pT_ready, 1)
                        pe.wait_ge(pT_copied, 1)
                        for b in range(NS):
                            i = NS + b
                            pe.wait_ge(kv_in[i % RING], 16 * (i // RING + 1))
                            for k in range(KT):
                                for a in range(2):
                                    c = NS * (k // 2) + b
                                    last = nc.tensor.matmul(ps[:, 7, NS * k + b:NS * k + b + 1], kv[:, i % RING, a, P * k:P * k + P],
                                                            pT[:, a, c:c + 1], start=(a == 0), stop=(a == 1))
                            last.then_inc(v_done, 1)

                    @block.scalar
                    def _(act):
                        act_c.eng = act
                        for b in range(NS):
                            act.wait_ge(k_turned, 2 * b + 1)
                            if b >= 2:
                                act.wait_ge(s_done, b - 1)
                            nc.scalar.activation(cT_[:, b % 2, 0:4, :].rearrange("p (b k) t -> p b (k t)", k=2), ps[:, 0:2, :],
                                                 ACT.Copy).then_inc(k_copied[0], 1)
                        act.wait_ge(neg_r, 1)
                        act_c(nc.scalar.activation(rows[:], rows[:], ACT.Exp, bias=st[:, 1:2], accum_out=st[:, 2:3]))
                        act.sem_inc(exp_r, 1)
                        act.wait_ge(v_done, NS)
                        nc.scalar.activation(hh[:, :, SEQ:T], ps[:, 7, 0:64].rearrange("p (k b) -> p k b", b=NS), ACT.Copy)\
                            .then_inc(hi_r, 1)

                    @block.vector
                    def _(dve):
                        dve_c.eng = dve
                        dve_c(nc.vector.tensor_copy(qs[:], Y[:, :, SEQ:T]))
                        dve.sem_inc(q_ready, 1)
                        for b in range(NS):
                            dve.wait_ge(k_turned, 2 * b + 2)
                            if b >= 2:
                                dve.wait_ge(s_done, b - 1)
                            nc.vector.tensor_copy(cT_[:, b % 2, 4:8, :].rearrange("p (b k) t -> p b (k t)", k=2), ps[:, 2:4, :])\
                                .then_inc(k_copied[1], 1)
                        dve.wait_ge(s_done, NS)
                        nc.vector.tensor_scalar(sT[:].rearrange("p a c -> p (a c)"), ps[:, 4, 0:64], 256 ** -0.5, None, ALU.mult)\
                            .then_inc(sT_ready, 1)
                        dve.wait_ge(rows_ready, 1)
                        dve_c(nc.vector.tensor_copy(rows[:], ps[0:32, 5, 0:NMEM]))
                        dve_c(nc.vector.tensor_reduce(st[:, 0:1], rows[:], AX.X, ALU.max))
                        nc.vector.tensor_scalar(st[:, 1:2], st[:, 0:1], -1.0, None, ALU.mult).then_inc(neg_r, 1)
                        dve.wait_ge(exp_r, 1)
                        dve_c(nc.vector.reciprocal(st[:, 3:4], st[:, 2:3]))
                        nc.vector.tensor_scalar(rows[:], rows[:], st[:, 3:4], None, ALU.mult).then_inc(p_r, 1)
                        dve.wait_ge(pT_ready, 1)
                        nc.vector.tensor_copy(pT[:].rearrange("p a c -> p (a c)"), ps[:, 6, 0:64]).then_inc(pT_copied, 1)
                        dve.wait_ge(hi_r, 1)
                        dve_c(nc.vector.tensor_tensor(hl[:, :, SEQ:T], ps[:, 7, 0:64].rearrange("p (k b) -> p k b", b=NS),
                                                      hh[:, :, SEQ:T].bitcast(F32), ALU.subtract))

        def stage_ffn(l):
            with ExitStack() as ph:
                cache = ph.enter_context(nc.sbuf_tensor("f_cache", [P, 2 * FT, 2 * NS], F32))
                tail = ph.enter_context(nc.sbuf_tensor("f_tail", [P, 2 * FT, 2 + NS], F32))
                cin, cturn, ckept = sem("fc_in"), sem("fc_turned"), sem("fc_kept")
                with ExitStack() as ph2:
                    crows = ph2.enter_context(nc.sbuf_tensor("f_cache_rows", [2 * NS, DFF], F32))
                    with nc.Block() as block:
                        @block.sync
                        def _(sp):
                            src = io["cache_ffn_conv"][l].rearrange("b t f -> (b t) f")
                            for h in range(2):
                                if h:
                                    sp.wait_ge(cturn, 1)
                                sp.dma_start(crows[:], src[:, DFF * h:DFF * h + DFF]).then_inc(cin, 16)
                            sp.dma_start(io["conv_sample"][l, :, 0, :], io["cache_ffn_conv"][l, :, 1, :]).then_inc(ckept, 16)
                            sp.wait_ge(ckept, 16)

                        @block.tensor
                        def _(pe):
                            for h in range(2):
                                pe.wait_ge(cin, 16 * (h + 1))
                                for j in range(FT):
                                    last = nc.tensor.transpose(ps[:, h, 16 * j:16 * j + 16], crows[:, P * j:P * j + P],
                                                               ident[0:16, 0:16])
                                last.then_inc(cturn, 1)

                        @block.vector
                        def _(dve):
                            dve_c.eng = dve
                            for h in range(2):
                                dve.wait_ge(cturn, h + 1)
                                dve_c(nc.vector.tensor_copy(cache[:, FT * h:FT * h + FT, :].rearrange("p k c -> p (k c)"),
                                                            ps[:, h, 0:16 * FT]))

                work = ph.enter_context(ExitStack())

                def tmp(name, shape, dt=F32):
                    return work.enter_context(nc.sbuf_tensor(name, shape, dt))

                U = tmp("f_u", [P, 2, 2 + T])
                C = tmp("f_c", [P, 2, T])
                gh, gl = tmp("f_ghi", [P, 2, T], F32R), tmp("f_glo", [P, 2, T], F32R)
                f_up, f_c0, f_conv, f_silu, f_g, f_gh, f_gl, f_down, f_y = (
                    sem(f"f_{n}") for n in ("up", "c0", "conv", "silu", "g", "gh", "gl", "down", "y"))
                DOWN_BANKS = (6, 7, 0, 1, 2)
                first_slab = {}
                for n, key in enumerate(ffn_order):
                    first_slab[key] = S_FFN + n
                with nc.Block() as block:
                    @block.sync
                    def _(sp):
                        load_slabs(sp, l, N_SLABS)

                    @block.gpsimd
                    def _(pool):
                        split_lo(pool, N_SLABS)

                    @block.tensor
                    def _(pe):
                        def down(j):
                            n = first_slab["d", j]
                            pe.wait_ge(lo_done, n + 1)
                            pe.wait_ge(f_gl, j + 1)
                            pe.wait_ge(f_up, 2 * min(j + 1, FT - 1) + 1)
                            s = n % 2
                            for f in range(KT):
                                for c in range(NCH):
                                    i = NCH * f + c
                                    m = 24 * j + i
                                    if m >= 5:
                                        pe.wait_ge(f_y, m - 4 if i >= 5 else 24 * j)
                                    last = mm3(ps[:, DOWN_BANKS[i % 5], 0:CH], w_hi[:, s, P * f:P * f + P], w_lo[:, s, P * f:P * f + P],
                                               gh[:, j % 2, CH * c:CH * c + CH], gl[:, j % 2, CH * c:CH * c + CH], True, True)
                                    last.then_inc(f_down if i < 23 else w_used, 1)

                        for j in range(FT):
                            for h, kind in enumerate("ab"):
                                if j:
                                    pe.wait_ge(f_up, 2 * (j - 1) + h + 1)
                                    if j >= 2:
                                        pe.wait_ge(f_y, 24 * (j - 1))
                                project(pe, first_slab[kind, j], 3 * h)
                            if j:
                                down(j - 1)
                        down(FT - 1)

                    @block.scalar
                    def _(act):
                        act_c.eng = act
                        for j in range(FT):
                            for h, kind in enumerate("ab"):
                                split_hi(act, first_slab[kind, j] + 2 + h)
                                act.wait_ge(f_up, 2 * j + h + 1)
                                if j:
                                    act.wait_ge(f_gl, j)
                                col = FT * h + j
                                nc.scalar.activation(C[:, h, :], U[:, h, 2:2 + T], ACT.Identity, bias=cT[:, 3, col:col + 1],
                                                     scale=cT[:, 2, col:col + 1]).then_inc(f_c0, 1)
                            act.wait_ge(f_conv, 2 * j + 1)
                            nc.scalar.activation(C[:, 0, :], C[:, 0, :], ACT.Silu).then_inc(f_silu, 1)
                            act.wait_ge(f_g, j + 1)
                            nc.scalar.activation(gh[:, j % 2, :], C[:, 1, :], ACT.Copy).then_inc(f_gh, 1)
                        split_hi(act, N_SLABS)

                    @block.vector
                    def _(dve):
                        dve_c.eng = dve
                        for h in range(2):
                            dve_c(nc.vector.memset(U[:, h, 0:2], 0.0))
                        ca = cache[:].rearrange("p k (b t) -> p k t b", t=2)

                        def up(j, h):
                            n = first_slab["ab"[h], j]
                            col = FT * h + j
                            dve.wait_ge(w_used, n + 1)
                            nc.vector.tensor_tensor(tokens3(U[:, h, 2:2 + T]), ps[:, 3 * h:3 * h + 3, 0:CH], tokens3(rs[:]),
                                                    ALU.mult).then_inc(f_up, 1)
                            dve.wait_ge(f_up, 2 * j + h + 1)
                            dve_c(nc.vector.tensor_copy(tail[:, col, :], U[:, h, SEQ:SEQ + 2 + NS]))
                            dve.wait_ge(f_c0, 2 * j + h + 1)
                            c = C[:, h, :]
                            for t in range(2):
                                w = cT[:, t, col:col + 1]
                                dve_c(nc.vector.scalar_tensor_tensor(c[:, 0:SEQ], U[:, h, t:t + SEQ], w, c[:, 0:SEQ],
                                                                     ALU.mult, ALU.add))
                                dve_c(nc.vector.scalar_tensor_tensor(c[:, SEQ:T], ca[:, col, t, :], w, c[:, SEQ:T],
                                                                     ALU.mult, ALU.add))
                            dve.sem_inc(f_conv, 1)

                        def gate(j):
                            dve.wait_ge(f_silu, j + 1)
                            nc.vector.tensor_tensor(C[:, 1, :], C[:, 0, :], C[:, 1, :], ALU.mult).then_inc(f_g, 1)
                            dve.wait_ge(f_gh, j + 1)
                            if j >= 2:
                                dve.wait_ge(w_used, first_slab["d", j - 2] + 1)
                            nc.vector.tensor_tensor(gl[:, j % 2, :], C[:, 1, :], gh[:, j % 2, :].bitcast(F32),
                                                    ALU.subtract).then_inc(f_gl, 1)

                        def add(j):
                            for f in range(KT):
                                for c in range(NCH):
                                    i = NCH * f + c
                                    if i < 23:
                                        dve.wait_ge(f_down, 23 * j + i + 1)
                                    else:
                                        dve.wait_ge(w_used, first_slab["d", j] + 1)
                                    y, b = Y[:, f, CH * c:CH * c + CH], ps[:, DOWN_BANKS[(NCH * f + c) % 5], 0:CH]
                                    if j == 0:
                                        nc.vector.tensor_copy(y, b).then_inc(f_y, 1)
                                    else:
                                        nc.vector.tensor_tensor(y, y, b, ALU.add).then_inc(f_y, 1)

                        for j in range(FT):
                            up(j, 0)
                            if j:
                                add(j - 1)
                            up(j, 1)
                            gate(j)
                        add(FT - 1)
                        dve.wait_ge(f_y, 24 * FT)

                work.close()
                with ExitStack() as ph2:
                    trow = ph2.enter_context(nc.sbuf_tensor("f_tail_rows", [2 + NS, 2, 2048], F32))
                    t_turn, t_copy, t_out = sem("ft_turned"), sem("ft_copied"), sem("ft_out")
                    with nc.Block() as block:
                        n_round = 3

                        def tiles(i):
                            return range(16 * i, min(16 * i + 16, 2 * FT))

                        @block.tensor
                        def _(pe):
                            for i in range(n_round):
                                if i >= 2:
                                    pe.wait_ge(t_copy, i - 1)
                                for k in tiles(i):
                                    b = 4 * (i % 2) + (k % 16) // 4
                                    last = nc.tensor.transpose(ps[0:2 + NS, b, P * (k % 4):P * (k % 4) + P], tail[:, k, :], ident[:])
                                last.then_inc(t_turn, 1)

                        @block.scalar
                        def _(act):
                            for i in range(n_round):
                                act.wait_ge(t_turn, i + 1)
                                if i >= 2:
                                    act.wait_ge(t_out, 32 * (i - 1))
                                nb = len(tiles(i)) // 4
                                nc.scalar.activation(trow[:, i % 2, 0:512 * nb].rearrange("p (b c) -> p b c", b=nb),
                                                     ps[0:2 + NS, 4 * (i % 2):4 * (i % 2) + nb, :], ACT.Copy).then_inc(t_copy, 1)

                        @block.sync
                        def _(sp):
                            for i in range(n_round):
                                sp.wait_ge(t_copy, i + 1)
                                w = P * len(tiles(i))
                                cs = slice(2048 * i, 2048 * i + w)
                                sp.dma_start(io["conv_prompt"][l, 0, :, cs], trow[0:2, i % 2, 0:w]).then_inc(t_out, 16)
                                sp.dma_start(io["conv_sample"][l, :, 1, cs], trow[2:2 + NS, i % 2, 0:w]).then_inc(t_out, 16)
                                sp.wait_ge(t_out, 32 * (i + 1))

        clear_semaphores(True)
        with nc.Fori(0, DEPTH) as l:
            stage_parameters(l)
            stage_norm("n0", l, None, G_PRE_MIX, 0)
            stage_hgrn(l)
            clear_semaphores(False)
            with ExitStack() as mix:
                q = mix.enter_context(nc.sbuf_tensor("q", [P, G, T], F32))
                kT = mix.enter_context(nc.sbuf_tensor("k", [P, T], F32))
                v = mix.enter_context(nc.sbuf_tensor("v", [P, T], F32))
                stage_qkv(l, q, kT, v)
                stage_window(l, q, kT, v)
            stage_project("wo", l, S_WO, N_WO, True, False)
            with ExitStack() as cross:
                mkT = cross.enter_context(nc.sbuf_tensor("mkT", [P, KT, NMEM], F32))
                mv = cross.enter_context(nc.sbuf_tensor("mv", [P, 2, D], F32))
                stage_memory(l, mkT, mv)
                stage_norm("n1", l, G_POST_MIX, G_PRE_X, S_XQ)
                stage_project("xq", l, S_XQ, N_XQ, False, True)
                stage_cross(l, mkT, mv)
            stage_cross_samples(l)
            stage_project("xo", l, S_XO, N_XO, False, False)
            clear_semaphores(False)
            stage_norm("n2", l, G_POST_X, G_PRE_FFN, S_FFN)
            stage_ffn(l)
            stage_norm("n3", l, G_POST_FFN, None, N_SLABS - 2)
            clear_semaphores(True)

        with ExitStack() as ph:
            yrow = ph.enter_context(nc.sbuf_tensor("y_rows", [P, 2, D], F32))
            y_turned, y_copied, y_out = sem("y_turned"), sem("y_copied"), sem("y_out")
            with nc.Block() as block:
                @block.tensor
                def _(pe):
                    for i in range(n_tiles):
                        m, _ = row_tile(i)
                        if i >= 2:
                            pe.wait_ge(y_copied, i - 1)
                        for k in range(KT):
                            last = nc.tensor.transpose(ps[0:m, 2 * (i % 2) + k // 4, P * (k % 4):P * (k % 4) + P],
                                                       xT[:, k, P * i:P * i + m], ident[:])
                        last.then_inc(y_turned, 1)

                @block.scalar
                def _(act):
                    for i in range(n_tiles):
                        m, _ = row_tile(i)
                        act.wait_ge(y_turned, i + 1)
                        if i >= 2:
                            act.wait_ge(y_out, 16 * (i - 1))
                        b = 2 * (i % 2)
                        nc.scalar.activation(yrow[0:m, i % 2, :].rearrange("p (b c) -> p b c", b=2), ps[0:m, b:b + 2, :],
                                             ACT.Copy).then_inc(y_copied, 1)

                @block.sync
                def _(sp):
                    for i in range(n_tiles):
                        m, _ = row_tile(i)
                        sp.wait_ge(y_copied, i + 1)
                        dst = io["y_prompt"][0, P * i:P * i + P, :] if i < NB else io["y_sample"][:, 0, :]
                        sp.dma_start(dst, yrow[0:m, i % 2, :]).then_inc(y_out, 16)
                        sp.wait_ge(y_out, 16 * (i + 1))


def constants():
    f = np.float32
    q, k = np.arange(P)[:, None], np.arange(2 * P)[None, :] - P
    diff = q - k
    swa = np.where((diff >= 0) & (diff <= WINDOW), f(0), f(NEG)).astype(f)
    s, t = np.arange(P)[:, None], np.arange(P)[None, :]
    lvl = np.zeros((P, LEVELS, P), f)
    for lv in range(1, LEVELS + 1):
        hf = 1 << (lv - 1)
        lvl[:, lv - 1] = (s // (2 * hf) == t // (2 * hf)) & (s % (2 * hf) < hf) & (t % (2 * hf) >= hf)
    inv = (10000.0 ** (-np.arange(ROPE_HALF) / ROPE_HALF)).astype(f)
    pos = np.concatenate([np.arange(SEQ), np.full(NS, PAST)]).astype(f)
    ang = (pos[None, :] * inv[:, None]).astype(f)
    cos, sin = np.cos(ang).astype(f), np.sin(ang).astype(f)
    return {
        "c_ident": np.eye(P, dtype=f),
        "c_swa": swa,
        "c_lvl": lvl,
        "c_cos": np.tile(cos, (4, 1)),
        "c_sin": np.concatenate([-sin, sin, -sin, sin], axis=0),
    }


_INS = ["x_prompt", "x_sample", "cache_win_k", "cache_win_v", "cache_mem_k", "cache_mem_v", "state_hgrn", "cache_ffn_conv",
        "mem_prompt", "w_in", "w_o", "attn_sinks", "lb_logits", "hgrn_norm", "w_xq", "w_xk", "w_xv", "w_xo", "w_up", "conv_w",
        "conv_b", "w_down", "g_pre_mix", "g_post_mix", "g_pre_x", "g_post_x", "g_mem", "g_pre_ffn", "g_post_ffn"]
_OUTS = [("y_prompt", (1, SEQ, D)), ("y_sample", (NS, 1, D)),
         ("win_k_prompt", (DEPTH, 1, WINDOW, NKV, HD)), ("win_v_prompt", (DEPTH, 1, WINDOW, NKV, HD)),
         ("win_k_sample", (DEPTH, NS, 1, NKV, HD)), ("win_v_sample", (DEPTH, NS, 1, NKV, HD)),
         ("mem_k_prompt", (DEPTH, 1, NMEM, XH, 256)), ("mem_v_prompt", (DEPTH, 1, NMEM, XH, 256)),
         ("hgrn_prompt", (DEPTH, 1, RH, P, P)), ("hgrn_sample", (DEPTH, NS, RH, P, P)),
         ("conv_prompt", (DEPTH, 1, 2, 2 * DFF)), ("conv_sample", (DEPTH, NS, 2, 2 * DFF))]


def kernel(**inputs):
    import concourse.bacc as bacc
    from concourse.bass_utils import run_bass_kernel_spmd

    nc = bacc.Bacc("TRN2", target_bir_lowering=False, num_devices=1)
    arrays, io = {}, {}
    for name, a in [(n, inputs[n]) for n in _INS] + list(constants().items()):
        a = np.ascontiguousarray(a)
        arrays[f"in_{name}"] = a
        io[name] = nc.dram_tensor(f"in_{name}", a.shape, mybir.dt.from_np(a.dtype), kind="ExternalInput").ap()
    for name, shape in _OUTS:
        io[name] = nc.dram_tensor(f"out_{name}", shape, F32, kind="ExternalOutput").ap()
    build_program(nc, io)
    r = run_bass_kernel_spmd(nc, [arrays], core_ids=[0])
    return tuple(r.results[0][f"out_{name}"] for name, _ in _OUTS)
```
